# Optimizing a Trainium2 kernel written in Bass

```python
import jax
import jax.numpy as jnp
from jax import lax
import numpy as np
import jax, jax.numpy as jnp

D_MODEL = 1024
BATCH = 1
SEQ = 256
DEPTH = 2

CHUNK = 64
N_MEM = 256
N_BRANCH = 5
BRANCH_WIDTH = D_MODEL // 2
N_HEADS = 4
HEAD_DIM = BRANCH_WIDTH // N_HEADS
SB_BLOCK = 128
GMLP_BLOCK = 128
GM_GROUPS = 4
CONV_WIDTH = 4
ROPE_BASE = 10000.0
EPS = 1e-6


def _in_sizes():
    w, h = BRANCH_WIDTH, N_HEADS
    return ([w] * 4
            + [w] * 5 + [h, h]
            + [w] * 3
            + [w] * 4
            + [w] * 2
            + [N_BRANCH * D_MODEL])

def rms_norm(x, g):
    xf = x.astype(jnp.float32)
    y = xf * lax.rsqrt(jnp.mean(xf * xf, axis=-1, keepdims=True) + EPS)
    return (y * g.astype(jnp.float32)).astype(x.dtype)

def layer_norm(x, g, b):
    xf = x.astype(jnp.float32)
    mu = jnp.mean(xf, axis=-1, keepdims=True)
    var = jnp.mean(jnp.square(xf - mu), axis=-1, keepdims=True)
    y = (xf - mu) * lax.rsqrt(var + EPS)
    return (y * g.astype(jnp.float32) + b.astype(jnp.float32)).astype(x.dtype)

def head_norm(t):
    tf = t.astype(jnp.float32)
    mu = jnp.mean(tf, axis=-1, keepdims=True)
    var = jnp.mean(jnp.square(tf - mu), axis=-1, keepdims=True)
    return (tf - mu) * lax.rsqrt(var + EPS)

def causal_conv(x, w):
    k = w.shape[0]
    return lax.conv_general_dilated(
        x, w[:, None, :].astype(x.dtype), window_strides=(1,), padding=((k - 1, 0),),
        dimension_numbers=('NWC', 'WIO', 'NWC'), feature_group_count=x.shape[-1])

def rotary(t, positions):
    half = t.shape[-1] // 2
    inv_freq = ROPE_BASE ** (-jnp.arange(half, dtype=jnp.float32) / half)
    ang = positions.astype(jnp.float32)[..., None] * inv_freq
    cos, sin = jnp.cos(ang)[:, :, None, :], jnp.sin(ang)[:, :, None, :]
    tf = t.astype(jnp.float32)
    t1, t2 = tf[..., :half], tf[..., half:]
    return jnp.concatenate([t1 * cos - t2 * sin, t1 * sin + t2 * cos], axis=-1)

def to_chunks(t):
    b, s, h = t.shape[:3]
    t = t.astype(jnp.float32).reshape(b, s // CHUNK, CHUNK, h, *t.shape[3:])
    return jnp.moveaxis(t, 3, 1)

def from_chunks(t):
    b, h, nc, l, d = t.shape
    return jnp.moveaxis(t, 1, 3).reshape(b, nc * l, h, d)

def stick_breaking(q, k, v):
    b, s, h, d = q.shape
    nb = s // SB_BLOCK
    qb = q.reshape(b, nb, SB_BLOCK, h, d).transpose(1, 0, 3, 2, 4)
    kf = k.transpose(0, 2, 1, 3).astype(jnp.float32)
    vf = v.transpose(0, 2, 1, 3).astype(jnp.float32)
    key_pos = jnp.arange(s)
    scale = d ** -0.5

    def block(args):
        q_blk, i = args
        z = jnp.einsum('bhqd,bhkd->bhqk', q_blk.astype(jnp.float32), kf) * scale
        q_pos = i * SB_BLOCK + jnp.arange(SB_BLOCK)
        valid = key_pos[None, :] < q_pos[:, None]
        log_keep = jnp.where(valid, -jax.nn.softplus(z), 0.0)
        later = lax.cumsum(log_keep, axis=3, reverse=True) - log_keep
        w = jnp.where(valid, jnp.exp(jax.nn.log_sigmoid(z) + later), 0.0)
        return jnp.einsum('bhqk,bhkd->bhqd', w, vf)

    out = lax.map(block, (qb, jnp.arange(nb)))
    return out.transpose(1, 0, 3, 2, 4).reshape(b, s, h, d).astype(q.dtype)

def mlstm(q, k, v, i_pre, f_pre):
    b_, s_, h_, d = q.shape
    qc, kc, vc = to_chunks(q), to_chunks(k) * d ** -0.5, to_chunks(v)
    ic = to_chunks(i_pre)
    bcum = jnp.cumsum(jax.nn.log_sigmoid(to_chunks(f_pre)), axis=-1)
    g = bcum + lax.cummax(ic - bcum, axis=3)
    b_last, a_last = bcum[..., -1], g[..., -1]
    w_end = jnp.exp(b_last[..., None] - bcum + ic - a_last[..., None])
    kv_loc = jnp.einsum('bhcld,bhcle->bhcde', kc * w_end[..., None], vc)
    n_loc = jnp.einsum('bhcl,bhcld->bhcd', w_end, kc)

    def step(carry, inp):
        c_st, n_st, m_st = carry
        bl, al, kv, nl = inp
        m_new = jnp.maximum(bl + m_st, al)
        d_old = jnp.exp(bl + m_st - m_new)
        d_loc = jnp.exp(al - m_new)
        c_new = d_old[..., None, None] * c_st + d_loc[..., None, None] * kv
        n_new = d_old[..., None] * n_st + d_loc[..., None] * nl
        return (c_new, n_new, m_new), (c_st, n_st, m_st)

    init = (jnp.zeros((b_, h_, d, d), jnp.float32), jnp.zeros((b_, h_, d), jnp.float32),
            jnp.zeros((b_, h_), jnp.float32))
    xs = (jnp.moveaxis(b_last, 2, 0), jnp.moveaxis(a_last, 2, 0),
          jnp.moveaxis(kv_loc, 2, 0), jnp.moveaxis(n_loc, 2, 0))
    _, (c_prev, n_prev, m_prev) = lax.scan(step, init, xs)
    c_prev = jnp.moveaxis(c_prev, 0, 2)
    n_prev = jnp.moveaxis(n_prev, 0, 2)
    m_prev = jnp.moveaxis(m_prev, 0, 2)

    m_t = jnp.maximum(bcum + m_prev[..., None], g)
    d_inter = jnp.exp(bcum + m_prev[..., None] - m_t)
    num = d_inter[..., None] * jnp.einsum('bhcld,bhcde->bhcle', qc, c_prev)
    den = d_inter * jnp.einsum('bhcld,bhcd->bhcl', qc, n_prev)
    causal = jnp.tril(jnp.ones((CHUNK, CHUNK), dtype=bool))
    log_d = bcum[..., :, None] - bcum[..., None, :] + ic[..., None, :] - m_t[..., :, None]
    d_intra = jnp.exp(jnp.where(causal, log_d, -jnp.inf))
    sc = jnp.einsum('bhctd,bhcsd->bhcts', qc, kc) * d_intra
    num = num + jnp.einsum('bhcts,bhcse->bhcte', sc, vc)
    den = den + jnp.sum(sc, axis=-1)
    h = num / jnp.maximum(jnp.abs(den), jnp.exp(-m_t))[..., None]
    return from_chunks(h)

def retention(q, k, v):
    b_, s_, h_, d = q.shape
    qc, kc, vc = to_chunks(q), to_chunks(k) * d ** -0.5, to_chunks(v)
    log_gamma = jnp.log(1.0 - 2.0 ** (-5.0 - jnp.arange(h_, dtype=jnp.float32)))
    idx = jnp.arange(CHUNK, dtype=jnp.float32)
    intra_decay = jnp.exp(log_gamma[:, None, None] * jnp.abs(idx[:, None] - idx[None, :]))
    sc = jnp.einsum('bhcnd,bhcmd->bhcnm', qc, kc) * intra_decay[:, None]
    intra = jnp.einsum('bhcnm,bhcme->bhcne', sc, vc)
    w_end = jnp.exp(log_gamma[:, None] * (CHUNK - 1 - idx))
    kv_loc = jnp.einsum('bhcld,bhcle->bhcde', kc * w_end[None, :, None, :, None], vc)
    chunk_decay = jnp.exp(log_gamma * CHUNK)[None, :, None, None]

    def step(state, kv):
        return chunk_decay * state + kv, state

    _, s_prev = lax.scan(step, jnp.zeros((b_, h_, d, d), jnp.float32), jnp.moveaxis(kv_loc, 2, 0))
    s_prev = jnp.moveaxis(s_prev, 0, 2)
    w_q = jnp.exp(log_gamma[:, None] * (idx + 1.0))
    inter = w_q[:, None, :, None] * jnp.einsum('bhcnd,bhcde->bhcne', qc, s_prev)
    return from_chunks(intra + inter)

def spatial_gating(u, v, ln_g, ln_b, w_s, b_s):
    b_, s_, w = u.shape
    v = layer_norm(v, ln_g, ln_b)
    vb = v.reshape(b_, s_ // GMLP_BLOCK, GMLP_BLOCK, GM_GROUPS, w // GM_GROUPS)
    chunk_id = jnp.arange(GMLP_BLOCK) // CHUNK
    mask = chunk_id[None, :] <= chunk_id[:, None]
    mixed = jnp.einsum('gpq,bnqgc->bnpgc', jnp.where(mask, w_s, 0.0).astype(v.dtype), vb)
    mixed = mixed + b_s.T[:, :, None].astype(v.dtype)
    return u * mixed.reshape(b_, s_, w)

def memory_attention(q, mem_k, mem_v):
    logits = jnp.einsum('bshd,bmhd->bhsm', q.astype(jnp.float32), mem_k.astype(jnp.float32))
    p = jax.nn.softmax(logits * q.shape[-1] ** -0.5, axis=-1)
    return jnp.einsum('bhsm,bmhd->bshd', p, mem_v.astype(jnp.float32)).astype(q.dtype)

def hybrid_layer(x, mem, positions, norm_pre, norm_post, w_in, b_igate, b_fgate, conv_q, conv_k,
                 gm_ln_g, gm_ln_b, gm_ws, gm_bs, mem_norm, w_mem_kv, w_up, w_out):
    b_, s_, _ = x.shape
    w = BRANCH_WIDTH
    heads = lambda t: t.reshape(t.shape[0], t.shape[1], N_HEADS, HEAD_DIM)
    flat = lambda t: t.reshape(b_, s_, w).astype(x.dtype)

    h = rms_norm(x, norm_pre)
    proj = h @ w_in
    split_points = [int(p) for p in np.cumsum(_in_sizes())[:-1]]
    (sb_q, sb_k, sb_v, sb_z,
     ml_q, ml_k, ml_v, ml_o, ml_z, ml_i, ml_f,
     gm_u, gm_v, gm_z,
     rt_q, rt_k, rt_v, rt_z,
     xa_q, xa_z, gates) = jnp.split(proj, split_points, axis=-1)

    y_sb = flat(stick_breaking(heads(sb_q), heads(sb_k), heads(sb_v)))
    q_ml = jax.nn.silu(causal_conv(ml_q, conv_q))
    k_ml = jax.nn.silu(causal_conv(ml_k, conv_k))
    h_ml = mlstm(heads(q_ml), heads(k_ml), heads(ml_v), ml_i + b_igate, ml_f + b_fgate)
    y_ml = flat(head_norm(h_ml)) * jax.nn.sigmoid(ml_o)
    y_gm = spatial_gating(jax.nn.gelu(gm_u), jax.nn.gelu(gm_v), gm_ln_g, gm_ln_b, gm_ws, gm_bs)
    y_rt = flat(head_norm(retention(rotary(heads(rt_q), positions), rotary(heads(rt_k), positions),
                                    heads(rt_v))))
    mkv = rms_norm(mem, mem_norm) @ w_mem_kv
    mem_k, mem_v = jnp.split(mkv, 2, axis=-1)
    y_xa = flat(memory_attention(heads(xa_q), heads(mem_k), heads(mem_v)))

    ys = jnp.stack([y_sb * jax.nn.silu(sb_z), y_ml * jax.nn.silu(ml_z), y_gm * jax.nn.silu(gm_z),
                    y_rt * jax.nn.silu(rt_z), y_xa * jax.nn.silu(xa_z)], axis=2)
    up = jnp.einsum('bsnw,nwd->bsnd', ys, w_up)
    merged = jnp.sum(jax.nn.sigmoid(gates.reshape(b_, s_, N_BRANCH, D_MODEL)) * up, axis=2)
    out = merged @ w_out
    return x + rms_norm(out, norm_post)

def first_inputs(seed: int = 0) -> dict:
    key = jax.random.key(seed)
    ks = jax.random.split(key, 20)
    f32 = jnp.float32
    nrm = lambda k, shape, scale: jax.random.normal(k, shape, f32) * scale
    w = BRANCH_WIDTH
    d_in = sum(_in_sizes())
    x = nrm(ks[0], (BATCH, SEQ, D_MODEL), 1.0)
    mem = nrm(ks[1], (BATCH, N_MEM, D_MODEL), 1.0)
    offset = jax.random.randint(ks[2], (BATCH, 1), 0, 4096, dtype=jnp.int32)
    positions = offset + jnp.arange(SEQ, dtype=jnp.int32)[None, :]
    norm_pre = 1.0 + nrm(ks[3], (DEPTH, D_MODEL), 0.02)
    norm_post = 1.0 + nrm(ks[4], (DEPTH, D_MODEL), 0.02)
    w_in = nrm(ks[5], (DEPTH, D_MODEL, d_in), D_MODEL ** -0.5)
    b_igate = nrm(ks[6], (DEPTH, N_HEADS), 0.1)
    b_fgate = jnp.linspace(3.0, 6.0, N_HEADS, dtype=f32)[None, :] + nrm(ks[7], (DEPTH, N_HEADS), 0.1)
    conv_q = nrm(ks[8], (DEPTH, CONV_WIDTH, w), CONV_WIDTH ** -0.5)
    conv_k = nrm(ks[9], (DEPTH, CONV_WIDTH, w), CONV_WIDTH ** -0.5)
    gm_ln_g = 1.0 + nrm(ks[10], (DEPTH, w), 0.02)
    gm_ln_b = nrm(ks[11], (DEPTH, w), 0.02)
    gm_ws = nrm(ks[12], (DEPTH, GM_GROUPS, GMLP_BLOCK, GMLP_BLOCK), GMLP_BLOCK ** -0.5)
    gm_bs = 1.0 + nrm(ks[13], (DEPTH, GM_GROUPS, GMLP_BLOCK), 0.02)
    mem_norm = 1.0 + nrm(ks[14], (DEPTH, D_MODEL), 0.02)
    w_mem_kv = nrm(ks[15], (DEPTH, D_MODEL, 2 * w), D_MODEL ** -0.5)
    w_up = nrm(ks[16], (DEPTH, N_BRANCH, w, D_MODEL), w ** -0.5)
    w_out = nrm(ks[17], (DEPTH, D_MODEL, D_MODEL), D_MODEL ** -0.5)
    return {"x": x, "mem": mem, "positions": positions, "norm_pre": norm_pre, "norm_post": norm_post,
            "w_in": w_in, "b_igate": b_igate, "b_fgate": b_fgate, "conv_q": conv_q, "conv_k": conv_k,
            "gm_ln_g": gm_ln_g, "gm_ln_b": gm_ln_b, "gm_ws": gm_ws, "gm_bs": gm_bs,
            "mem_norm": mem_norm, "w_mem_kv": w_mem_kv, "w_up": w_up, "w_out": w_out}

def first_block(x, mem, positions, norm_pre, norm_post, w_in, b_igate, b_fgate, conv_q, conv_k,
              gm_ln_g, gm_ln_b, gm_ws, gm_bs, mem_norm, w_mem_kv, w_up, w_out):
    for l in range(DEPTH):
        x = hybrid_layer(x, mem, positions, norm_pre[l], norm_post[l], w_in[l], b_igate[l], b_fgate[l],
                         conv_q[l], conv_k[l], gm_ln_g[l], gm_ln_b[l], gm_ws[l], gm_bs[l],
                         mem_norm[l], w_mem_kv[l], w_up[l], w_out[l])
    return x


_first_inputs = first_inputs


def first_inputs(seed=0):
    import zlib

    import numpy as np

    out = dict(_first_inputs(seed))
    spreads = {}
    factors = {'b_igate': 8.0, 'gm_ln_g': 7.293, 'gm_ln_b': 6.949, 'gm_bs': 6.163, 'mem_norm': 8.0}
    for name, (base, spread) in spreads.items():
        noise = np.random.default_rng([zlib.crc32(name.encode()), seed]).standard_normal(out[name].shape)
        drawn = base * np.exp(spread * noise) if base else spread * noise
        out[name] = jnp.asarray(drawn.astype(out[name].dtype))
    for name, factor in factors.items():
        out[name] = (out[name] * factor).astype(out[name].dtype)
    return out


_narrow_inputs = first_inputs


def first_inputs(seed=0):
    out = dict(_narrow_inputs(seed))
    wider = {'b_igate': 12.0, 'gm_ln_g': 5.15, 'gm_ln_b': 5.38, 'gm_bs': 5.19}
    for name, times in wider.items():
        mean = out[name].mean()
        out[name] = (mean + times * (out[name] - mean)).astype(out[name].dtype)
    return out


XA_HEADS = 4
XA_HD = D_MODEL // XA_HEADS
W_A = D_MODEL
H_A = 8
HD_A = W_A // H_A
CONV_A = 4
C_RG = 8.0
W_B = D_MODEL // 2
POOL_WINDOWS = (2, 4, 8, 16)
G_B = len(POOL_WINDOWS)
HD_B = W_B // G_B
IN_AB = 2 * W_A + W_B
OUT_AB = W_A + W_B
CONV_C = 31
D_FF = 3 * D_MODEL
CONV_F = 3
N_EVEN = (DEPTH + 1) // 2
N_ODD = DEPTH // 2


def rms_norm_2(x, g):
    xf = x.astype(jnp.float32)
    y = xf * lax.rsqrt(jnp.mean(xf * xf, axis=-1, keepdims=True) + EPS)
    return (y * g.astype(jnp.float32)).astype(x.dtype)

def layer_norm_2(x, g, b):
    xf = x.astype(jnp.float32)
    mu = jnp.mean(xf, axis=-1, keepdims=True)
    var = jnp.mean(jnp.square(xf - mu), axis=-1, keepdims=True)
    y = (xf - mu) * lax.rsqrt(var + EPS)
    return (y * g.astype(jnp.float32) + b.astype(jnp.float32)).astype(x.dtype)

def causal_dwconv(x, w, b):
    K, C = w.shape
    y = lax.conv_general_dilated(
        x, w[:, None, :], window_strides=(1,), padding=[(K - 1, 0)],
        dimension_numbers=("NWC", "WIO", "NWC"), feature_group_count=C)
    return y + b

def rg_lru(x, w_gx, b_gx, w_ga, b_ga, lam):
    Bn, S, W = x.shape
    xh = x.reshape(Bn, S, H_A, HD_A)
    gate_x = jax.nn.sigmoid(jnp.einsum('bshi,hij->bshj', xh, w_gx).reshape(Bn, S, W) + b_gx)
    gate_a = jax.nn.sigmoid(jnp.einsum('bshi,hij->bshj', xh, w_ga).reshape(Bn, S, W) + b_ga)
    log_a = -C_RG * gate_a.astype(jnp.float32) * jax.nn.softplus(-lam.astype(jnp.float32))
    a = jnp.exp(log_a)
    mult = jnp.sqrt(-jnp.expm1(2.0 * log_a))
    bx = mult * (gate_x * x).astype(jnp.float32)

    def combine(lhs, rhs):
        a_l, b_l = lhs
        a_r, b_r = rhs
        return a_l * a_r, a_r * b_l + b_r

    _, h = lax.associative_scan(combine, (a, bx), axis=1)
    return h.astype(x.dtype)

def multi_scale_pool(u, w_g, b_g, scale):
    Bn, S, W = u.shape
    uf = u.astype(jnp.float32)
    csum = jnp.cumsum(uf, axis=1)
    t = jnp.arange(1, S + 1, dtype=jnp.float32)[:, None]
    outs = []
    for g, w in enumerate(POOL_WINDOWS):
        sl = slice(g * HD_B, (g + 1) * HD_B)
        cg = csum[..., sl]
        lagged = jnp.pad(cg[:, :S - w], ((0, 0), (w, 0), (0, 0)))
        mean = (cg - lagged) / jnp.minimum(t, float(w))
        outs.append(mean - uf[..., sl])
    p = jnp.stack(outs, axis=2).astype(u.dtype)
    y = jnp.einsum('bsgi,gij->bsgj', p, w_g).reshape(Bn, S, W) + b_g
    return y * scale

def mixer_ab(x, norm, w_in, conv_w, conv_b, w_gx, b_gx, w_ga, b_ga, lam, w_pool, b_pool, pool_scale, w_out):
    z = rms_norm_2(x, norm) @ w_in
    z_gate = z[..., :W_A]
    z_rec = z[..., W_A:2 * W_A]
    z_pool = z[..., 2 * W_A:]
    xr = causal_dwconv(z_rec, conv_w, conv_b)
    y_a = jax.nn.gelu(z_gate) * rg_lru(xr, w_gx, b_gx, w_ga, b_ga, lam)
    y_b = multi_scale_pool(z_pool, w_pool, b_pool, pool_scale)
    return jnp.concatenate([y_a, y_b], axis=-1) @ w_out

def conformer_conv(x, norm, w1, b1, dw_w, dw_b, ln_g, ln_b, w2, b2):
    h = rms_norm_2(x, norm) @ w1 + b1
    h = jax.nn.glu(h, axis=-1)
    h = causal_dwconv(h, dw_w, dw_b)
    h = jax.nn.silu(layer_norm_2(h, ln_g, ln_b))
    return h @ w2 + b2

def cross_attn(x, mem, norm, mem_norm, wq, wk, wv, wo):
    Bn, S, _ = x.shape
    M = mem.shape[1]
    q = (rms_norm_2(x, norm) @ wq).reshape(Bn, S, XA_HEADS, XA_HD)
    m = rms_norm_2(mem, mem_norm)
    k = (m @ wk).reshape(Bn, M, XA_HEADS, XA_HD)
    v = (m @ wv).reshape(Bn, M, XA_HEADS, XA_HD)
    s = jnp.einsum('bqhd,bkhd->bhqk', q, k).astype(jnp.float32) * (XA_HD ** -0.5)
    p = jax.nn.softmax(s, axis=-1).astype(x.dtype)
    o = jnp.einsum('bhqk,bkhd->bqhd', p, v).reshape(Bn, S, D_MODEL)
    return o @ wo

def conv_ffn(x, norm, w_up, dw_w, dw_b, w_down):
    h = rms_norm_2(x, norm) @ w_up
    g = causal_dwconv(h[..., :D_FF], dw_w, dw_b)
    u = h[..., D_FF:]
    return (jax.nn.gelu(g) * u) @ w_down

def second_inputs(seed: int = 0) -> dict:
    key = jax.random.key(seed)
    keys = iter(jax.random.split(key, 48))

    def nrm(shape, scale):
        return jax.random.normal(next(keys), shape, jnp.float32) * scale

    def gain(shape):
        return 1.0 + 0.02 * jax.random.normal(next(keys), shape, jnp.float32)

    L, NE, NO, D = DEPTH, N_EVEN, N_ODD, D_MODEL
    u = jax.random.uniform(next(keys), (NE, W_A), jnp.float32, 0.9, 0.999) ** (1.0 / C_RG)
    lam = jnp.log(u) - jnp.log1p(-u)
    return {
        "x": jax.random.normal(next(keys), (BATCH, SEQ, D), jnp.float32),
        "mem": jax.random.normal(next(keys), (BATCH, N_MEM, D), jnp.float32),
        "ab_norm": gain((NE, D)),
        "ab_w_in": nrm((NE, D, IN_AB), D ** -0.5),
        "a_conv_w": nrm((NE, CONV_A, W_A), CONV_A ** -0.5),
        "a_conv_b": nrm((NE, W_A), 0.01),
        "a_gate_x_w": nrm((NE, H_A, HD_A, HD_A), HD_A ** -0.5),
        "a_gate_x_b": nrm((NE, W_A), 0.01),
        "a_gate_a_w": nrm((NE, H_A, HD_A, HD_A), HD_A ** -0.5),
        "a_gate_a_b": nrm((NE, W_A), 0.01),
        "a_lambda": lam,
        "b_group_w": nrm((NE, G_B, HD_B, HD_B), HD_B ** -0.5),
        "b_group_b": nrm((NE, W_B), 0.01),
        "b_scale": 1.0 + 0.1 * jax.random.normal(next(keys), (NE, W_B), jnp.float32),
        "ab_w_out": nrm((NE, OUT_AB, D), OUT_AB ** -0.5),
        "c_norm": gain((NO, D)),
        "c_w_pw1": nrm((NO, D, 2 * D), D ** -0.5),
        "c_b_pw1": nrm((NO, 2 * D), 0.01),
        "c_dw_w": nrm((NO, CONV_C, D), CONV_C ** -0.5),
        "c_dw_b": nrm((NO, D), 0.01),
        "c_ln_g": gain((NO, D)),
        "c_ln_b": nrm((NO, D), 0.01),
        "c_w_pw2": nrm((NO, D, D), D ** -0.5),
        "c_b_pw2": nrm((NO, D), 0.01),
        "xa_norm": gain((L, D)),
        "xa_mem_norm": gain((L, D)),
        "xa_wq": nrm((L, D, D), D ** -0.5),
        "xa_wk": nrm((L, D, D), D ** -0.5),
        "xa_wv": nrm((L, D, D), D ** -0.5),
        "xa_wo": nrm((L, D, D), D ** -0.5),
        "f_norm": gain((L, D)),
        "f_w_up": nrm((L, D, 2 * D_FF), D ** -0.5),
        "f_dw_w": nrm((L, CONV_F, D_FF), CONV_F ** -0.5),
        "f_dw_b": nrm((L, D_FF), 0.01),
        "f_w_down": nrm((L, D_FF, D), D_FF ** -0.5),
        "final_norm": gain((D,)),
    }

def second_block(x, mem, ab_norm, ab_w_in, a_conv_w, a_conv_b, a_gate_x_w, a_gate_x_b,
              a_gate_a_w, a_gate_a_b, a_lambda, b_group_w, b_group_b, b_scale, ab_w_out,
              c_norm, c_w_pw1, c_b_pw1, c_dw_w, c_dw_b, c_ln_g, c_ln_b, c_w_pw2, c_b_pw2,
              xa_norm, xa_mem_norm, xa_wq, xa_wk, xa_wv, xa_wo,
              f_norm, f_w_up, f_dw_w, f_dw_b, f_w_down, final_norm):
    for layer in range(DEPTH):
        if layer % 2 == 0:
            i = layer // 2
            x = x + mixer_ab(x, ab_norm[i], ab_w_in[i], a_conv_w[i], a_conv_b[i],
                             a_gate_x_w[i], a_gate_x_b[i], a_gate_a_w[i], a_gate_a_b[i],
                             a_lambda[i], b_group_w[i], b_group_b[i], b_scale[i], ab_w_out[i])
        else:
            j = layer // 2
            x = x + conformer_conv(x, c_norm[j], c_w_pw1[j], c_b_pw1[j], c_dw_w[j], c_dw_b[j],
                                   c_ln_g[j], c_ln_b[j], c_w_pw2[j], c_b_pw2[j])
        x = x + cross_attn(x, mem, xa_norm[layer], xa_mem_norm[layer], xa_wq[layer],
                           xa_wk[layer], xa_wv[layer], xa_wo[layer])
        x = x + conv_ffn(x, f_norm[layer], f_w_up[layer], f_dw_w[layer], f_dw_b[layer],
                         f_w_down[layer])
    return rms_norm_2(x, final_norm)


def setup_inputs(seed=0):
    out = dict(first_inputs(seed))
    for name, value in second_inputs(seed + 1).items():
        if name != "x":
            out[name + "_2"] = value
    return out


def reference(
    x, mem, positions, norm_pre, norm_post, w_in, b_igate, b_fgate, conv_q, conv_k, gm_ln_g,
    gm_ln_b, gm_ws, gm_bs, mem_norm, w_mem_kv, w_up, w_out, mem_2, ab_norm_2, ab_w_in_2,
    a_conv_w_2, a_conv_b_2, a_gate_x_w_2, a_gate_x_b_2, a_gate_a_w_2, a_gate_a_b_2, a_lambda_2,
    b_group_w_2, b_group_b_2, b_scale_2, ab_w_out_2, c_norm_2, c_w_pw1_2, c_b_pw1_2, c_dw_w_2,
    c_dw_b_2, c_ln_g_2, c_ln_b_2, c_w_pw2_2, c_b_pw2_2, xa_norm_2, xa_mem_norm_2, xa_wq_2,
    xa_wk_2, xa_wv_2, xa_wo_2, f_norm_2, f_w_up_2, f_dw_w_2, f_dw_b_2, f_w_down_2, final_norm_2,
):
    x = first_block(
        x, mem, positions, norm_pre, norm_post, w_in, b_igate, b_fgate, conv_q, conv_k, gm_ln_g,
        gm_ln_b, gm_ws, gm_bs, mem_norm, w_mem_kv, w_up, w_out,
    )
    return second_block(
        x, mem_2, ab_norm_2, ab_w_in_2, a_conv_w_2, a_conv_b_2, a_gate_x_w_2, a_gate_x_b_2,
        a_gate_a_w_2, a_gate_a_b_2, a_lambda_2, b_group_w_2, b_group_b_2, b_scale_2, ab_w_out_2,
        c_norm_2, c_w_pw1_2, c_b_pw1_2, c_dw_w_2, c_dw_b_2, c_ln_g_2, c_ln_b_2, c_w_pw2_2,
        c_b_pw2_2, xa_norm_2, xa_mem_norm_2, xa_wq_2, xa_wk_2, xa_wv_2, xa_wo_2, f_norm_2,
        f_w_up_2, f_dw_w_2, f_dw_b_2, f_w_down_2, final_norm_2,
    )


_drawn_inputs = setup_inputs


def setup_inputs(seed=0):
    import zlib

    import numpy as np

    out = dict(_drawn_inputs(seed))
    spreads = {}
    factors = {'ab_norm_2': 6.898,
     'a_conv_b_2': 4.79,
     'a_gate_x_b_2': 8.0,
     'a_gate_a_b_2': 8.0,
     'b_group_b_2': 8.0,
     'c_norm_2': 25.709,
     'c_b_pw1_2': 47.451,
     'c_dw_b_2': 36.162,
     'c_ln_g_2': 33.012,
     'c_ln_b_2': 64.0,
     'c_b_pw2_2': 52.904,
     'xa_norm_2': 8.0,
     'xa_mem_norm_2': 8.0,
     'f_norm_2': 4.029,
     'f_dw_b_2': 8.0,
     'final_norm_2': 7.738}
    for name, (base, spread) in spreads.items():
        noise = np.random.default_rng([zlib.crc32(name.encode()), seed]).standard_normal(out[name].shape)
        drawn = base * np.exp(spread * noise) if base else spread * noise
        out[name] = jnp.asarray(drawn.astype(out[name].dtype))
    for name, factor in factors.items():
        out[name] = (out[name] * factor).astype(out[name].dtype)
    return out
```

```python
import concourse.bass as bass
import numpy as np
from concourse import mybir
from contextlib import ExitStack

F32 = mybir.dt.float32
I32 = mybir.dt.int32
ACT = mybir.ActivationFunctionType
ALU = mybir.AluOpType
AX = mybir.AxisListType

P = 128
S, D = 256, 1024
NT, KD = S // P, D // P
DEPTH = 2
W = D // 2
H, HD = 4, P
EPS = 1e-6
BIG = 1e30
RING = 3
BANKS = 8
FF = 3 * D
KF = FF // P
TRI = 3 * P

SBQ, SBK, SBV, SBZ = (i * W for i in range(4))
MLQ, MLK, MLV, MLO, MLZ = (4 * W + i * W for i in range(5))
MLI = 9 * W
MLF = MLI + H
GMU, GMV, GMZ = (MLF + H + i * W for i in range(3))
RTQ, RTK, RTV, RTZ = (GMZ + W + i * W for i in range(4))
XAQ, XAZ = RTZ + W, RTZ + 2 * W
GATE = XAZ + W

C_ID, C_TRI, C_LKM, C_NB, C_MLN, C_GMM = 0, 128, 256, 640, 1024, 1152
C_DEC, C_INV, C_ONE, C_SEL, C_RC = 1280, 2304, 2368, 2496, 3008
C_ALL = C_RC + 4 * S


def constants():
    c = np.zeros((P, C_ALL), np.float32)
    i, j = np.arange(P)[:, None], np.arange(P)[None, :]
    c[:, C_ID:C_ID + P] = i == j
    c[:, C_TRI:C_TRI + P] = i >= j
    for at, inner, valid, other in ((C_LKM, -1.0, 0.0, -1.0), (C_NB, 0.0, -BIG, 0.0)):
        for o in (0, 2 * P):
            c[:, at + o:at + o + P] = np.where(i < j, inner, valid)
        c[:, at + P:at + 2 * P] = other
    c[:, C_MLN:C_MLN + P] = np.where(i <= j, 0.0, -BIG)
    c[:, C_GMM:C_GMM + P] = i // 64 <= j // 64
    gamma = np.log(1.0 - 2.0 ** (-5.0 - np.arange(H)))
    for h in range(H):
        at = C_DEC + 2 * P * h
        c[:, at:at + P] = np.where(i // 64 <= j // 64, np.exp(gamma[h] * np.abs(i - j)), 0) * HD ** -0.5
        c[:, at + P:at + 2 * P] = np.exp(gamma[h] * (j + P - i)) * HD ** -0.5
        c[h, C_SEL + h * P:C_SEL + (h + 1) * P] = 1.0
        c[:, C_RC + h * S:C_RC + (h + 1) * S] = 1.0 / np.minimum(np.arange(1, S + 1), 2 ** (h + 1))
    c[:, C_INV:C_INV + 64] = np.float32(10000.0) ** (-np.arange(64, dtype=np.float32) / np.float32(64))
    c[:, C_ONE:C_ONE + P] = 1.0
    return c


class Count:

    def __init__(self, known, now):
        self.known, self.marks, self.n, self.now = known, {}, 0, now

    @property
    def stage(self):
        return self.now[0]

    def enter(self, stage, restart=False):
        self.now[0] = stage
        if restart:
            self.n = 0

    def __call__(self, *names):
        self.n += 1
        for name in names:
            assert (self.stage, name) not in self.marks, name
            self.marks[self.stage, name] = self.n
        return 1

    def at(self, name, stage=None):
        if self.known is None:
            return 1
        return self.known[stage or self.stage, name]

    def has(self, name):
        return self.known is not None and (self.stage, name) in self.known


def build(nc, A, out, known):
    kn = known or [None] * 4
    now = [None]
    PC, SC, VC, GC = (Count(kn[i], now) for i in range(4))
    ctx = ExitStack()
    with ctx:
        def sb(name, shape, dt=F32):
            return ctx.enter_context(nc.sbuf_tensor(name, shape, dt))

        def sem(name):
            return ctx.enter_context(nc.semaphore(name))

        xs = sb("x_tokens", [P, NT, D])
        hT = sb("h_features", [P, KD, S])
        memT = sb("mem_features", [P, KD, S])
        ring = sb("weight_ring", [P, RING, 4096])
        arena = sb("arena", [P, 26, 1024])
        cst = sb("constants_sb", [P, C_ALL])
        wsT = sb("spatial_weights", [P, 4, P])
        rows = sb("vector_rows", [P, P])
        cols = sb("vector_columns", [P, 52])
        cols2 = sb("vector_columns_2", [P, 616])
        brow = sb("row_vectors", [P, 2048])
        trig = sb("cos_sin", [P, 2, NT, 64])
        pos_i = sb("positions_int", [P, NT], I32)
        pos_f = sb("positions_float", [P, NT])
        bif = sb("gate_biases", [H, 2])
        gr = arena[0:H, 23:25, :].rearrange("p a (r s) -> p (a r) s", s=S)
        st = sb("statistics", [P, 16, 8])
        bst = sb("bn_statistics", [P, 2, 8])
        lam = sb("lambda_columns", [P, 4, 8])
        epsc = sb("eps_column", [P, 1])
        ps = [ctx.enter_context(nc.psum_tensor(f"bank{i}", [P, 512], F32)) for i in range(BANKS)]

        pe_done, act_done, vec_done, pool_done = (sem(n) for n in ("pe_done", "act_done", "vec_done", "pool_done"))
        slot_full = [sem(f"slot{i}_full") for i in range(RING)]
        slot_free = [sem(f"slot{i}_free") for i in range(RING)]
        const_in, x_in, mem_in, small_in = sem("const_in"), sem("x_in"), sem("mem_in"), sem("small_in")
        small2_in, rows2_in, out_done = sem("small2_in"), sem("rows2_in"), sem("out_done")
        arrived, go, spare = sem("layer_arrived"), sem("layer_go"), sem("spare")

        def sec(i, n=1):
            return arena[:, i:i + n, :].rearrange("p a n -> p (a n)")

        def tok(i):
            return arena[:, i, :].rearrange("p (t n) -> p t n", t=NT)

        def tok4(i):
            return arena[:, i, :].rearrange("p (t h n) -> p t h n", t=NT, h=H)

        def feat(i, n=1):
            return sec(i, n).rearrange("p (j s) -> p j s", s=S)

        def con(at, n=P):
            return cst[:, at:at + n]

        ident, ones = con(C_ID), con(C_ONE)

        def two(*names):
            return [(n, i) for n in names for i in range(2)]

        def four(*names):
            return [(n, i) for n in names for i in range(4)]

        GATES = lambda b: four(f"gate{b}") + [(f"yT{b}", 0), (f"yT{b}", 1)] + four(f"up{b}")
        ORDER = {
            "pro": four("memT"),
            "L": ([("cols", 0)] + four("hT") + two("sbq", "sbk", "sbv", "sbz", "mk", "mv") + four("sbs")
                  + two("mlq", "mlk") + four("sbw") + two("mlv", "mlo", "mlz") + [("mlif", 0)]
                  + two("sby", "rtq", "rtk", "rtv", "rtz") + [("mle", 0)] + four("mld", "mls")
                  + two("gmu", "gmv") + [("mln", 0)] + two("mly", "gmz") + two("rqT", "rkT") + four("rts")
                  + [("wsT", 0)] + two("xaq", "xaz", "rty") + four("xas") + two("gmy")
                  + GATES(0) + four("xap") + GATES(1) + two("xay") + GATES(2) + GATES(3) + GATES(4)
                  + four("mgT", "o")),
            "AB": ([("cols2", i) for i in range(2)] + four("memT", "hT") + four("rec", "ga", "gx") + four("gate")
                   + two("pu", "pl") + four("o")),
            "C": four("hT", "cb", "ca") + two("mu", "var") + four("o"),
        }
        for s in range(DEPTH):
            ORDER[f"X{s}"] = four("hT", "q", "k", "v", "s", "p", "oT", "o")
            ORDER[f"F{s}"] = (four("hT") + [("o", i) for i in range(4)]
                              + [g for j in range(6) for g in two(f"g{j}", f"u{j}")])
        HELD = {"sbw": "sbs"}

        PLACE, BEFORE = {}, {}
        for stage, order in ORDER.items():
            last = {}
            g = 0
            for name, i in order:
                if name in HELD:
                    PLACE[stage, name, i] = PLACE[stage, HELD[name], i]
                    last[PLACE[stage, name, i]] = (name, i)
                    continue
                if stage[0] == "F" and name != "hT":
                    b = 4 + i if name == "o" else g % 4
                else:
                    b = g % BANKS
                PLACE[stage, name, i] = b
                BEFORE[stage, name, i] = last.get(b)
                last[b] = (name, i)
                g += 1

        def bank(C, name, i=0):
            return ps[PLACE[C.stage, name, i]]

        def halves(b):
            return b[:, :].rearrange("p (j s) -> p j s", j=2)

        def quarters(b):
            return b[:, :].rearrange("p (h n) -> p h n", h=4)

        def kmaj(ap):
            return ap.rearrange("(k p) n -> p k n", p=P)

        def layer_chunks(l):
            win = kmaj(A["w_in"][l])
            wm = kmaj(A["w_mem_kv"][l])
            def w(c):
                return win[:, :, c:c + W]
            def u(b):
                return [w(GATE + b * D), w(GATE + b * D + W), kmaj(A["w_up"][l, b])]
            out_w = kmaj(A["w_out"][l])
            return ([w(SBQ), w(SBK), w(SBV), w(SBZ), wm[:, :, 0:W], wm[:, :, W:2 * W], w(MLQ), w(MLK), w(MLV), w(MLO),
                     w(MLZ), win[:, :, MLI:MLI + 2 * H], w(RTQ), w(RTK), w(RTV), w(RTZ), w(GMU), w(GMV), w(GMZ),
                     A["gm_ws"][l].rearrange("g p q -> p g q"), w(XAQ), w(XAZ)]
                    + u(0) + u(1) + u(2) + u(3) + u(4) + [out_w[:, :, 0:W], out_w[:, :, W:D]])

        LAYER_CHUNKS = 39
        def half(ap, c):
            return ap[:, :, c * W:(c + 1) * W]
        ab = kmaj(A["ab_w_in_2"][0])
        abo = kmaj(A["ab_w_out_2"][0])
        c1, c2 = kmaj(A["c_w_pw1_2"][0]), kmaj(A["c_w_pw2_2"][0])
        def gates_w(n):
            return A[n][0].rearrange("h i j -> i h j")
        ab_chunks = ([half(ab, 2), half(ab, 3), gates_w("a_gate_a_w_2"), gates_w("a_gate_x_w_2"), half(ab, 0), half(ab, 1),
                      half(ab, 4), gates_w("b_group_w_2")] + [abo[:, 4 * i:4 * i + 4, :] for i in range(3)])
        def xa_chunks(l):
            return [half(kmaj(A[n][l]), c) for n in ("xa_wq_2", "xa_wk_2", "xa_wv_2", "xa_wo_2") for c in range(2)]
        def ff_chunks(l):
            up, dn = kmaj(A["f_w_up_2"][l]), kmaj(A["f_w_down_2"][l])
            got = []
            for j in range(6):
                got += [half(up, j), half(up, 6 + j)]
                if j:
                    got.append(dn[:, 4 * j - 4:4 * j, :])
            return got + [dn[:, 20:24, :]]
        c_chunks = [half(c1, 2), half(c1, 3), half(c1, 0), half(c1, 1), half(c2, 0), half(c2, 1)]
        rest = ab_chunks + xa_chunks(0) + ff_chunks(0) + c_chunks + xa_chunks(1) + ff_chunks(1)

        block = ctx.enter_context(nc.Block())

        @block.sync
        def _(sp):
            sp.dma_start(cst[:, :], A["constants"]).then_inc(const_in, 16)
            sp.dma_start(xs[:, :, :], A["x"][0].rearrange("(t p) d -> p t d", p=P)).then_inc(x_in, 16)

            def load(n, src, l=None):
                s = n % RING
                before = n // RING + 1 if l is None else l * (LAYER_CHUNKS // RING) + n // RING + 1
                sp.wait_ge(slot_free[s], before)
                if l is not None:
                    sp.sem_inc(spare, 1)
                k, m = src.shape[1], src.shape[2]
                dst = ring[:, s, 0:k * m].rearrange("p (k m) -> p k m", k=k)
                if m < 64:
                    with nc.allow_non_contiguous_dma(reason="eight gate columns"):
                        sp.dma_start(dst, src).then_inc(slot_full[s], 16)
                else:
                    sp.dma_start(dst, src).then_inc(slot_full[s], 16)

            with sp.Fori(0, DEPTH) as l:
                chunks = layer_chunks(l)
                assert len(chunks) == LAYER_CHUNKS
                for n, src in enumerate(chunks):
                    load(n, src, l)
            for n, src in enumerate(rest):
                load(n + DEPTH * LAYER_CHUNKS, src)
            sp.wait_ge(vec_done, VC.at("final", "F1") if known else 1)
            sp.dma_start(out[0].rearrange("(t p) d -> p t d", p=P),
                         sec(0, 2).rearrange("p (t d) -> p t d", t=NT)).then_inc(out_done, 16)
            sp.wait_ge(out_done, 16)

        @block.gpsimd
        def _(pool):
            GC.enter("pro")

            def link(ins, *names):
                ins.then_inc(pool_done, GC(*names))
                pool.wait_ge(pool_done, GC.n)

            def mem_gain(col, dst, c):
                for k in range(KD):
                    ins = nc.gpsimd.tensor_scalar(dst[:, k, :], memT[:, k, :], c[:, col + k:col + k + 1], None, ALU.mult)
                ins.then_inc(pool_done, GC("mTg"))

            nc.gpsimd.memset(epsc[:, :], EPS).then_inc(pool_done, GC("eps"))
            pool.dma_start(arena[:, 0:2, :], A["mem"][0].rearrange("(t p) d -> p t d", p=P)).then_inc(mem_in, 16)
            with nc.allow_non_contiguous_dma(reason="one position per partition"):
                pool.dma_start(pos_i[:, :], A["positions"][0].rearrange("(t p) -> p t", p=P)).then_inc(mem_in, 16)
            with pool.Fori(0, DEPTH) as l:
                GC.enter("L", True)
                r128 = "(r c) -> r c"
                pool.wait_ge(go, l + 1)
                pool.sem_inc(spare, 1)
                for src, r0, n in ((A["norm_pre"][l].rearrange(r128, c=P), 0, 8),
                                   (A["mem_norm"][l].rearrange(r128, c=P), 8, 8),
                                   (A["conv_q"][l].rearrange("k (r c) -> (k r) c", c=P), 16, 16),
                                   (A["conv_k"][l].rearrange("k (r c) -> (k r) c", c=P), 32, 16),
                                   (A["gm_bs"][l], 48, 4)):
                    pool.dma_start(rows[r0:r0 + n, :], src).then_inc(small_in, 16)
                for n, name in enumerate(("b_igate", "b_fgate")):
                    with nc.allow_non_contiguous_dma(reason="one bias per partition"):
                        pool.dma_start(bif[:, n:n + 1], A[name][l].rearrange("(h a) -> h a", a=1)).then_inc(small_in, 16)
                for name, o, n in (("norm_post", 0, D), ("gm_ln_g", D, W), ("gm_ln_b", D + W, W)):
                    pool.dma_start(brow[:, o:o + n], A[name][l].rearrange("(a n) -> a n", a=1).to_broadcast([P, n])).then_inc(small2_in, 16)
                pool.wait_ge(act_done, SC.at("cols"))
                mem_gain(8, feat(15, 2), cols)
                pool.wait_ge(act_done, SC.at("mlz"))
                nc.gpsimd.tensor_tensor(sec(10), sec(10), sec(9), ALU.mult).then_inc(pool_done, GC("mloz"))
                pool.wait_ge(pool_done, GC.n)
                pool.sem_inc(arrived, 1)
                pool.wait_ge(arrived, (l + 1) * 4)
                pool.sem_inc(spare, 1)
                for s in (pe_done, act_done, vec_done, pool_done):
                    pool.sem_clear(s)
                pool.sem_inc(go, 1)
            GC.enter("AB", True)
            pool.wait_ge(go, DEPTH + 1)
            pool.sem_inc(spare, 1)
            R = lambda t: arena[:, 20, t * P:(t + 1) * P]
            r128 = "(r c) -> r c"
            todo = []
            def put(t, r, ap):
                todo.append((R(t)[r:r + ap.shape[0], :], ap))
            at = 0
            for name in ("ab_norm_2", "a_conv_w_2", "a_conv_b_2", "a_gate_x_b_2", "a_gate_a_b_2", "a_lambda_2",
                         "b_group_b_2", "b_scale_2"):
                ap = A[name][0]
                ap = ap.rearrange("k (r c) -> (k r) c", c=P) if len(ap.shape) == 2 else ap.rearrange(r128, c=P)
                put(0, at, ap)
                at += ap.shape[0]
            assert at == 80
            at = 0
            for name in ("c_norm_2", "c_b_pw1_2", "c_dw_b_2", "c_ln_g_2", "c_ln_b_2"):
                ap = A[name][0].rearrange(r128, c=P)
                put(1, at, ap)
                at += ap.shape[0]
            dw = A["c_dw_w_2"][0].rearrange("k (r c) -> (k r) c", c=P)
            put(2, 0, dw[0:124, :])
            put(3, 0, dw[124:248, :])
            for l in range(DEPTH):
                at = 0
                for name in ("xa_norm_2", "xa_mem_norm_2", "f_norm_2", "f_dw_w_2", "f_dw_b_2"):
                    ap = A[name][l]
                    ap = ap.rearrange("k (r c) -> (k r) c", c=P) if len(ap.shape) == 2 else ap.rearrange(r128, c=P)
                    put(4 + l, at, ap)
                    at += ap.shape[0]
                assert at == 120
            for dst, src in todo:
                pool.dma_start(dst, src).then_inc(rows2_in, 16)
            pool.dma_start(arena[:, 0:2, :], A["mem_2"][0].rearrange("(t p) d -> p t d", p=P)).then_inc(mem_in, 16)
            pool.dma_start(brow[:, 0:D], A["c_b_pw2_2"].to_broadcast([P, D])).then_inc(mem_in, 16)
            pool.dma_start(brow[:, D:2 * D], A["final_norm_2"].rearrange("(a d) -> a d", a=1).to_broadcast([P, D]))\
                .then_inc(mem_in, 16)
            assert len(todo) * 16 == ROWS2
            for l in range(DEPTH):
                GC.enter(f"X{l}")
                pool.wait_ge(vec_done, VC.at("end", "AB" if l == 0 else "C"))
                pool.wait_ge(act_done, SC.at("end", "AB" if l == 0 else "C"))
                pool.wait_ge(pe_done, PC.at("end", "AB" if l == 0 else "C"))
                mem_gain(COL_F[l] + 8, feat(12, 2), cols2)

        @block.scalar
        def _(act):
            def link(ins, *names):
                ins.then_inc(act_done, SC(*names))
                act.wait_ge(act_done, SC.n)

            def filled(name, i=0):
                act.wait_ge(pe_done, PC.at((name, i)))
                return bank(SC, name, i)

            def copy(dst, name, i, func=ACT.Copy, *marks, view=None, **kw):
                b = filled(name, i)
                link(nc.scalar.activation(dst, (view(b) if view else b[:, :]), func, **kw), ("free", name, i), *marks)

            def rstd(name, n):
                act.wait_ge(vec_done, VC.at(name + ".ms"))
                link(nc.scalar.activation(st[:, 1, 0:n], st[:, 0, 0:n], ACT.Ln))
                link(nc.scalar.activation(st[:, 1, 0:n], st[:, 1, 0:n], ACT.Exp, scale=-0.5), name + ".rstd")

            def sums(src, name):
                for t in range(NT):
                    link(nc.scalar.activation(sec(25), src[:, t, :], ACT.Square, accum_out=st[:, 0, t:t + 1]),
                         *([name + ".ss"] if t else []))

            def norm_T(col, c, name="h"):
                sums(xs, name)
                rstd(name, NT)
                for i in range(4):
                    b = halves(filled("hT", i))
                    for j in range(2):
                        k = 2 * i + j
                        link(nc.scalar.activation(hT[:, k, :], b[:, j, :], ACT.Copy, scale=c[:, col + k:col + k + 1]),
                             *([("free", "hT", i), "hT%d" % i] if j else []))

            SC.enter("pro")
            act.wait_ge(mem_in, 32)
            act.wait_ge(pool_done, GC.at("eps", "pro"))
            m = arena[:, 0:2, :]
            sums(m, "mem")
            rstd("mem", NT)
            act.wait_ge(vec_done, VC.at("trig.in"))
            link(nc.scalar.activation(trig[:, :, :, :], arena[:, 4, 0:256].rearrange("p (a t n) -> p a t n", a=2, t=2),
                                      ACT.Sin), "trig")
            for i in range(4):
                copy(memT[:, 2 * i:2 * i + 2, :], "memT", i, view=halves)
            act.wait_ge(x_in, 16)
            act.wait_ge(pe_done, PC.at("end"))
            act.wait_ge(vec_done, VC.at("end"))
            act.sem_inc(arrived, 1)
            act.wait_ge(arrived, 3)
            act.sem_clear(act_done)
            act.sem_clear(pe_done)
            act.sem_clear(vec_done)
            act.sem_clear(pool_done)
            act.sem_clear(arrived)
            act.sem_inc(go, 1)

            with act.Fori(0, DEPTH) as l:
                SC.enter("L", True)
                act.wait_ge(go, l + 1)
                act.sem_inc(spare, 1)
                copy(cols[:, :], "cols", 0, ACT.Copy, "cols", view=lambda b: b[:, 0:52])
                norm_T(0, cols)
                for i in range(2):
                    copy(feat(0)[:, 2 * i:2 * i + 2, :], "sbq", i, ACT.Copy, f"sbq{i}", view=halves, scale=HD ** -0.5)
                for i in range(2):
                    copy(feat(1)[:, 2 * i:2 * i + 2, :], "sbk", i, ACT.Copy, f"sbk{i}", view=halves)
                for t in range(NT):
                    copy(tok(2)[:, t, :], "sbv", t, ACT.Copy, f"sbv{t}")
                for t in range(NT):
                    copy(tok(3)[:, t, :], "sbz", t, ACT.Silu, f"sbz{t}")
                for i in range(2):
                    copy(feat(4)[:, 2 * i:2 * i + 2, :], "mk", i, ACT.Copy, f"mk{i}", view=halves)
                for t in range(NT):
                    copy(tok(5)[:, t, :], "mv", t, ACT.Copy, f"mv{t}")
                sbr = sec(13, 2)
                for h in range(H):
                    e = sbr[:, h * TRI:(h + 1) * TRI]
                    b = filled("sbs", h)
                    link(nc.scalar.activation(e, b[:, 0:TRI], ACT.Abs))
                    link(nc.scalar.activation(e, e, ACT.Exp, scale=-1.0))
                    link(nc.scalar.activation(e, e, ACT.Ln, bias=1.0), f"sbln{h}")
                for n, (name, s) in enumerate((("mlq", 11), ("mlk", 12))):
                    for i in range(2):
                        b = halves(filled(name, i))
                        for j in range(2):
                            ft = 2 * i + j
                            c = 16 + 16 * n + 12 + ft
                            link(nc.scalar.activation(feat(s)[:, ft, :], b[:, j, :], ACT.Copy, scale=cols[:, c:c + 1]),
                                 f"{name}.tap{ft}")
                for h in range(H):
                    e = sbr[:, h * TRI:(h + 1) * TRI]
                    act.wait_ge(vec_done, VC.at(f"sblog{h}"))
                    link(nc.scalar.activation(e, e, ACT.Exp), f"sbw{h}")
                for name, s in (("mlq", 11), ("mlk", 12)):
                    act.wait_ge(vec_done, VC.at(name + ".conv"))
                    link(nc.scalar.activation(sec(s), sec(s), ACT.Silu), name)
                for t in range(NT):
                    copy(tok(8)[:, t, :], "mlv", t, ACT.Copy, f"mlv{t}")
                for t in range(NT):
                    copy(tok(9)[:, t, :], "mlo", t, ACT.Sigmoid)
                for t in range(NT):
                    copy(tok(10)[:, t, :], "mlz", t, ACT.Silu, *(["mlz"] if t else []))
                act.wait_ge(vec_done, VC.at("mlf"))
                link(nc.scalar.activation(gr[:, 1, :], gr[:, 0, :], ACT.Abs))
                link(nc.scalar.activation(gr[:, 1, :], gr[:, 1, :], ACT.Exp, scale=-1.0))
                link(nc.scalar.activation(gr[:, 1, :], gr[:, 1, :], ACT.Ln, bias=1.0), "mlf.ln")
                for name, s in (("rtq", 0), ("rtk", 1)):
                    for t in range(NT):
                        copy(tok(s)[:, t, :], name, t, ACT.Copy, f"{name}{t}")
                for t in range(NT):
                    copy(tok(6)[:, t, :], "rtv", t, ACT.Copy, f"rtv{t}")
                for t in range(NT):
                    copy(tok(7)[:, t, :], "rtz", t, ACT.Silu, f"rtz{t}")
                b = filled("mle")
                link(nc.scalar.activation(st[:, 2, :], b[:, 0:8], ACT.Exp))
                link(nc.scalar.activation(st[:, 3, :], b[:, 8:16], ACT.Copy), ("free", "mle", 0), "mlem")
                mlr = sec(15, 2)
                for h in range(H):
                    b = filled("mld", h)
                    o = h * TRI
                    link(nc.scalar.activation(mlr[:, o:o + S], b[:, 0:S], ACT.Exp, bias=st[:, 3, h:h + 1]))
                    link(nc.scalar.activation(mlr[:, o + S:o + TRI], b[:, S:TRI], ACT.Exp, bias=st[:, 3, H + h:H + h + 1]),
                         ("free", "mld", h), f"mld{h}")
                for name, s in (("gmu", 19), ("gmv", 20)):
                    for t in range(NT):
                        copy(tok(s)[:, t, :], name, t, ACT.Gelu_apprx_tanh, f"{name}{t}")

                def head_norm(name):
                    act.wait_ge(vec_done, VC.at(name + ".cen"))
                    link(nc.scalar.activation(sec(25), sec(22), ACT.Square), name + ".sq")
                    rstd(name, 8)

                copy(st[:, 3, :], "mln", 0, ACT.Abs, "mln.abs", view=lambda b: b[:, 0:8])
                head_norm("ml")
                for t in range(NT):
                    copy(tok(21)[:, t, :], "gmz", t, ACT.Silu, f"gmz{t}")
                for name, s in (("rqT", 0), ("rkT", 1)):
                    for i in range(2):
                        copy(feat(s)[:, 2 * i:2 * i + 2, :], name, i, ACT.Copy, f"{name}{i}", view=halves)
                rstd("gm", 2)
                for i in range(2):
                    copy(feat(2)[:, 2 * i:2 * i + 2, :], "xaq", i, ACT.Copy, f"xaq{i}", view=halves)
                for t in range(NT):
                    copy(tok(17)[:, t, :], "xaz", t, ACT.Silu, f"xaz{t}")
                head_norm("rt")
                pr = sec(15, 2)
                for h in range(H):
                    act.wait_ge(vec_done, VC.at(f"xamax{h}"))
                    b = filled("xas", h)
                    for t in range(NT):
                        link(nc.scalar.activation(pr[:, h * 512 + t * S:h * 512 + (t + 1) * S], b[:, t * S:(t + 1) * S], ACT.Exp,
                                                  scale=HD ** -0.5, bias=st[:, 4, 2 * h + t:2 * h + t + 1],
                                                  accum_out=st[:, 5, 2 * h + t:2 * h + t + 1]),
                             *([("free", "xas", h), f"xae{h}"] if t else []))

                def gates(b):
                    g = sec(8 if b % 2 == 0 else 19, 2).rearrange("p (t n) -> p t n", t=NT)
                    if b >= 2:
                        act.wait_ge(vec_done, VC.at(f"merge{b - 2}"))
                    elif b == 0:
                        act.wait_ge(pool_done, GC.at("mloz"))
                    else:
                        act.wait_ge(vec_done, VC.at("gmy"))
                    for i in range(4):
                        n, t = divmod(i, 2)
                        copy(g[:, t, n * 512:(n + 1) * 512], f"gate{b}", i, ACT.Sigmoid, *([f"gate{b}"] if i == 3 else []))
                    for i in range(2):
                        copy(feat(23 + b % 2)[:, 2 * i:2 * i + 2, :], f"yT{b}", i, ACT.Copy, *([f"yT{b}"] if i else []), view=halves)

                gates(0)
                for h in range(H):
                    copy(sec(13, 2)[:, h * 512:(h + 1) * 512], "xap", h, ACT.Copy, f"xap{h}")
                for b in range(1, 5):
                    gates(b)
                for i in range(4):
                    copy(feat(0, 2)[:, 2 * i:2 * i + 2, :], "mgT", i, ACT.Copy, *(["mgT"] if i == 3 else []), view=halves)
                o = sec(6, 2).rearrange("p (t n) -> p t n", t=NT)
                for i in range(4):
                    n, t = divmod(i, 2)
                    copy(o[:, t, n * 512:(n + 1) * 512], "o", i, ACT.Copy)
                sums(o, "post")
                rstd("post", NT)
                act.wait_ge(act_done, SC.n)
                act.sem_inc(arrived, 1)

            def plain_norm(col, name="h"):
                norm_T(col, cols2, name)

            SC.enter("AB", True)
            act.wait_ge(go, DEPTH + 1)
            act.sem_inc(spare, 1)
            for i, (c, n) in enumerate(((0, COL_F[1]), (COL_F[1], 120))):
                b = filled("cols2", i)
                link(nc.scalar.activation(cols2[:, c:c + n], b[:, 0:n], ACT.Copy), ("free", "cols2", i), f"cols2{i}")
            act.wait_ge(mem_in, 5 * 16)
            sums(arena[:, 0:2, :], "mem")
            rstd("mem", NT)
            for i in range(4):
                copy(memT[:, 2 * i:2 * i + 2, :], "memT", i, ACT.Copy, *(["memT"] if i == 3 else []), view=halves)
            link(nc.scalar.activation(lam[:, 0, :], cols2[:, COL_AB + 64:COL_AB + 72], ACT.Abs))
            link(nc.scalar.activation(lam[:, 0, :], lam[:, 0, :], ACT.Exp, scale=-1.0))
            link(nc.scalar.activation(lam[:, 0, :], lam[:, 0, :], ACT.Ln, bias=1.0), "lam.ln")
            plain_norm(COL_AB)
            for i in range(4):
                b = halves(filled("rec", i))
                for j in range(2):
                    ft = 2 * i + j
                    link(nc.scalar.activation(feat(2, 2)[:, ft, :], b[:, j, :], ACT.Identity,
                                              scale=cols2[:, COL_AB + 8 + 24 + ft:COL_AB + 8 + 25 + ft],
                                              bias=cols2[:, COL_AB + 40 + ft:COL_AB + 41 + ft]), f"rec.tap{ft}")
            for name, s, c in (("ga", 6, COL_AB + 56), ("gx", 4, COL_AB + 48)):
                for i in range(4):
                    b = halves(filled(name, i))
                    for j in range(2):
                        ft = 2 * i + j
                        link(nc.scalar.activation(feat(s, 2)[:, ft, :], b[:, j, :], ACT.Sigmoid, bias=cols2[:, c + ft:c + ft + 1]),
                             *([("free", name, i), f"{name}{i}"] if j else []))
            act.wait_ge(vec_done, VC.at("lam"))
            for k in range(KD):
                link(nc.scalar.activation(feat(8, 2)[:, k, :], feat(6, 2)[:, k, :], ACT.Tanh, scale=lam[:, 3, k:k + 1]))
            for k in range(KD):
                link(nc.scalar.activation(feat(6, 2)[:, k, :], feat(6, 2)[:, k, :], ACT.Exp, scale=lam[:, 2, k:k + 1]),
                     *(["a"] if k == KD - 1 else []))
            act.wait_ge(vec_done, VC.at("mult2"))
            link(nc.scalar.activation(sec(8, 2), sec(8, 2), ACT.Sqrt), "mult")
            for i in range(4):
                copy(feat(0, 2)[:, 2 * i:2 * i + 2, :], "gate", i, ACT.Gelu_apprx_tanh, *(["gate"] if i == 3 else []), view=halves)
            for i in range(2):
                copy(feat(12)[:, 2 * i:2 * i + 2, :], "pu", i, ACT.Copy, *(["pu"] if i else []), view=halves)
            link(nc.scalar.activation(epsc[:, :], epsc[:, :], ACT.Copy), "end")

            def cross(l):
                SC.enter(f"X{l}")
                act.wait_ge(vec_done, VC.at("end", "AB" if l == 0 else "C"))
                plain_norm(COL_F[l])
                for name, s in (("q", 0), ("k", 2)):
                    for i in range(4):
                        copy(feat(s, 2)[:, 2 * i:2 * i + 2, :], name, i, ACT.Copy, *([name] if i == 3 else []), view=halves)
                v = sec(4, 2).rearrange("p (t n) -> p t n", t=NT)
                for i in range(4):
                    n, t = divmod(i, 2)
                    copy(v[:, t, n * 512:(n + 1) * 512], "v", i, ACT.Copy, *(["v"] if i == 3 else []))
                pr = sec(6, 2)
                for h in range(H):
                    act.wait_ge(vec_done, VC.at(f"max{h}"))
                    b = filled("s", h)
                    for t in range(NT):
                        link(nc.scalar.activation(pr[:, h * 512 + t * S:h * 512 + (t + 1) * S], b[:, t * S:(t + 1) * S], ACT.Exp,
                                                  scale=1.0 / 16, bias=st[:, 4, 2 * h + t:2 * h + t + 1],
                                                  accum_out=st[:, 5, 2 * h + t:2 * h + t + 1]),
                             *([("free", "s", h), f"e{h}"] if t else []))
                for h in range(H):
                    copy(sec(8, 2)[:, h * 512:(h + 1) * 512], "p", h, ACT.Copy, f"pT{h}")
                for h in range(H):
                    copy(feat(10, 2)[:, 2 * h:2 * h + 2, :], "oT", h, ACT.Copy, *(["oT"] if h == 3 else []), view=halves)

            def ffn(l):
                SC.enter(f"F{l}")
                act.wait_ge(vec_done, VC.at("end", f"X{l}"))
                plain_norm(COL_F[l] + 16)
                w0, b0 = COL_F[l] + 24, COL_F[l] + 96
                for j in range(6):
                    c = feat(6 + j % 2)
                    if j >= 2:
                        act.wait_ge(vec_done, VC.at(f"h{j - 2}"))
                    for i in range(2):
                        b = halves(filled(f"g{j}", i))
                        for q in range(2):
                            f, ft = 2 * i + q, 4 * j + 2 * i + q
                            link(nc.scalar.activation(c[:, f, :], b[:, q, :], ACT.Identity, scale=cols2[:, w0 + 48 + ft:w0 + 49 + ft],
                                                      bias=cols2[:, b0 + ft:b0 + ft + 1]), f"tap{ft}")
                    act.wait_ge(vec_done, VC.at(f"conv{j}"))
                    link(nc.scalar.activation(sec(6 + j % 2), sec(6 + j % 2), ACT.Gelu_apprx_tanh), f"gelu{j}")

            cross(0)
            ffn(0)
            SC.enter("C")
            act.wait_ge(vec_done, VC.at("end", "F0"))
            plain_norm(COL_C)
            for i in range(4):
                b = halves(filled("cb", i))
                for j in range(2):
                    ft = 2 * i + j
                    c = COL_C + 16 + ft
                    link(nc.scalar.activation(feat(0, 2)[:, ft, :], b[:, j, :], ACT.Sigmoid, bias=cols2[:, c:c + 1]),
                         *([("free", "cb", i), f"cb{i}"] if j else []))
            w0 = COL_C + 48
            for ft in range(KD):
                act.wait_ge(vec_done, VC.at(f"glu{ft}"))
                link(nc.scalar.activation(feat(4, 2)[:, ft, :], feat(2, 2)[:, ft, :], ACT.Identity,
                                          scale=cols2[:, w0 + 240 + ft:w0 + 241 + ft], bias=cols2[:, COL_C + 24 + ft:COL_C + 25 + ft]),
                     f"tap{ft}")
            act.wait_ge(vec_done, VC.at("cen"))
            link(nc.scalar.activation(sec(8, 2), sec(6, 2), ACT.Square), "sq")
            act.wait_ge(vec_done, VC.at("var"))
            link(nc.scalar.activation(sec(13)[:, 0:S], sec(13)[:, 0:S], ACT.Ln))
            link(nc.scalar.activation(sec(13)[:, 0:S], sec(13)[:, 0:S], ACT.Exp, scale=-0.5), "rstd")
            act.wait_ge(vec_done, VC.at("xhat"))
            for ft in range(KD):
                link(nc.scalar.activation(feat(10, 2)[:, ft, :], feat(6, 2)[:, ft, :], ACT.Silu,
                                          scale=cols2[:, COL_C + 32 + ft:COL_C + 33 + ft], bias=cols2[:, COL_C + 40 + ft:COL_C + 41 + ft]),
                     *(["silu"] if ft == KD - 1 else []))
            link(nc.scalar.activation(epsc[:, :], epsc[:, :], ACT.Copy), "end")
            cross(1)
            ffn(1)
            act.wait_ge(vec_done, VC.at("res"))
            sums(xs, "fin")
            rstd("fin", NT)

        @block.vector
        def _(dve):
            def link(ins, *names):
                ins.then_inc(vec_done, VC(*names))
                dve.wait_ge(vec_done, VC.n)

            tt, ts, stt = nc.vector.tensor_tensor, nc.vector.tensor_scalar, nc.vector.scalar_tensor_tensor

            def filled(name, i=0):
                dve.wait_ge(pe_done, PC.at((name, i)))
                return bank(VC, name, i)

            def mean_square(name, n, width):
                dve.wait_ge(act_done, SC.at(name + ".ss"))
                link(ts(st[:, 0, 0:n], st[:, 0, 0:n], 1.0 / width, EPS, ALU.mult, ALU.add), name + ".ms")

            def normalise(src, dst, name, mark):
                mean_square(name, NT, D)
                dve.wait_ge(act_done, SC.at(name + ".rstd"))
                for t in range(NT):
                    link(ts(dst[:, t, :], src[:, t, :], st[:, 1, t:t + 1], None, ALU.mult), *([mark] if t else []))

            VC.enter("pro")
            xn = arena[:, 23:25, :]
            normalise(arena[:, 0:2, :], arena[:, 2:4, :], "mem", "mem.n")
            dve.wait_ge(mem_in, 32)
            dve.wait_ge(const_in, 16)
            link(nc.vector.tensor_copy(pos_f[:, :], pos_i[:, :]))
            ang, n, r = (arena[:, 5, a * 128:(a + 1) * 128].rearrange("p (t n) -> p t n", t=2) for a in range(3))
            cs = arena[:, 4, 0:256].rearrange("p (a t n) -> p a t n", a=2, t=2)
            for t in range(NT):
                link(ts(ang[:, t, :], con(C_INV, 64), pos_f[:, t:t + 1], None, ALU.mult))
            MAGIC = 1.5 * 2.0 ** 23
            link(ts(n, ang, float(1 / (2 * np.pi)), MAGIC, ALU.mult, ALU.add))
            link(ts(n, n, MAGIC, None, ALU.subtract))
            c1_ = 6.28125
            c2_ = float(np.float32(np.round((2 * np.pi - c1_) * 2 ** 20) / 2 ** 20))
            c3_ = float(2 * np.pi - c1_ - c2_)
            link(stt(r, n, -c1_, ang, ALU.mult, ALU.add))
            link(stt(r, n, -c2_, r, ALU.mult, ALU.add))
            link(stt(r, n, -c3_, r, ALU.mult, ALU.add))
            PI = 3.1415925
            link(ts(cs[:, 1], r, PI, -PI, ALU.min, ALU.max))
            link(ts(r, r, float(np.pi / 2), None, ALU.add))
            link(ts(n, r, float(np.pi), float(-2 * np.pi), ALU.is_gt, ALU.mult))
            link(tt(r, r, n, ALU.add))
            link(ts(cs[:, 0], r, PI, -PI, ALU.min, ALU.max), "trig.in")
            dve.wait_ge(act_done, SC.at("trig"))
            link(ts(pos_f[:, :], pos_f[:, :], 1.0, None, ALU.mult), "end")
            dve.sem_inc(arrived, 1)

            with dve.Fori(0, DEPTH) as l:
                VC.enter("L", True)
                dve.wait_ge(go, l + 1)
                dve.sem_inc(spare, 1)
                normalise(xs, xn, "h", "xn")
                sbr = sec(13, 2)
                for h in range(H):
                    e = sbr[:, h * TRI:(h + 1) * TRI]
                    b = bank(VC, "sbs", h)
                    dve.wait_ge(act_done, SC.at(f"sbln{h}"))
                    link(stt(e, b[:, 0:TRI], 0.0, e, ALU.max, ALU.add))
                    link(tt(e, e, con(C_LKM, TRI), ALU.mult), f"sblk{h}")
                for n, (name, s) in enumerate((("mlq", 11), ("mlk", 12))):
                    for i in range(2):
                        b = halves(filled(name, i))
                        for j in range(2):
                            ft = 2 * i + j
                            dve.wait_ge(act_done, SC.at(f"{name}.tap{ft | 1}"))
                            for d in range(1, 4):
                                c = 16 + 16 * n + 4 * (3 - d) + ft
                                y = feat(s)[:, ft, d:S]
                                marks = [("free", name, i)] if d == 3 and j == 1 else []
                                if marks and i == 1:
                                    marks.append(name + ".conv")
                                link(stt(y, b[:, j, 0:S - d], cols[:, c:c + 1], y, ALU.mult, ALU.add), *marks)
                for h in range(H):
                    e = sbr[:, h * TRI:(h + 1) * TRI]
                    b = filled("sbw", h)
                    link(stt(e, b[:, 0:TRI], 0.0, con(C_NB, TRI), ALU.min, ALU.add), f"sblog{h}", ("free", "sbw", h))
                b = filled("mlif")
                dve.wait_ge(small_in, (l + 1) * (7 * 16))
                link(ts(gr[:, 0, :], b[0:H, S:2 * S], bif[:, 1:2], None, ALU.add), "mlf")
                link(ts(gr[:, 2, :], b[0:H, 0:S], bif[:, 0:1], None, ALU.add), ("free", "mlif", 0))
                dve.wait_ge(act_done, SC.at("mlf.ln"))
                link(stt(gr[:, 0, :], gr[:, 0, :], 0.0, gr[:, 1, :], ALU.min, ALU.subtract))
                link(ts(gr[:, 1, :], gr[:, 0, :], 0.0, 1.0, ALU.mult, ALU.add))
                link(nc.vector.tensor_tensor_scan(gr[:, 3, :], gr[:, 1, :], gr[:, 0, :], 0.0, ALU.mult, ALU.add))
                link(tt(gr[:, 4, :], gr[:, 2, :], gr[:, 3, :], ALU.subtract))
                link(nc.vector.tensor_tensor_scan(gr[:, 5, :], gr[:, 4, :], gr[:, 4, :], 0.0, ALU.max, ALU.max))
                link(ts(gr[:, 6, :], gr[:, 5, :], -1.0, None, ALU.mult))
                link(tt(gr[:, 7, :], gr[:, 6, :], gr[:, 3, :], ALU.subtract), "mlrows")
                for t in range(NT):
                    b = filled("sby", t)
                    dve.wait_ge(act_done, SC.at(f"sbz{t}"))
                    link(tt(tok(3)[:, t, :], b[:, :], tok(3)[:, t, :], ALU.mult), ("free", "sby", t), f"y0{t}")
                cosv, sinv = (trig[:, a].unsqueeze(2).to_broadcast([P, NT, H, 64]) for a in range(2))
                for name, s, d in (("rtq", 0, 17), ("rtk", 1, 18)):
                    dve.wait_ge(act_done, SC.at(name + "1"))
                    x1, x2 = tok4(s)[:, :, :, 0:64], tok4(s)[:, :, :, 64:128]
                    y1, y2 = tok4(d)[:, :, :, 0:64], tok4(d)[:, :, :, 64:128]
                    t1, t2 = tok4(22)[:, :, :, 0:64], tok4(22)[:, :, :, 64:128]
                    for t in range(NT):
                        link(tt(t1[:, t], x2[:, t], sinv[:, t], ALU.mult))
                        link(tt(y1[:, t], x1[:, t], cosv[:, t], ALU.mult))
                        link(tt(y1[:, t], y1[:, t], t1[:, t], ALU.subtract))
                        link(tt(t2[:, t], x2[:, t], cosv[:, t], ALU.mult))
                        link(tt(y2[:, t], x1[:, t], sinv[:, t], ALU.mult))
                        link(tt(y2[:, t], y2[:, t], t2[:, t], ALU.add), *([name + "r"] if t else []))
                mlr = sec(15, 2)
                for h in range(H):
                    e = mlr[:, h * TRI:(h + 1) * TRI]
                    b = filled("mls", h)
                    dve.wait_ge(act_done, SC.at(f"mld{h}"))
                    link(stt(e, b[:, 0:TRI], HD ** -0.5, e, ALU.mult, ALU.mult), f"mlsc{h}", ("free", "mls", h))
                dve.wait_ge(act_done, SC.at("mln.abs"))
                link(tt(st[:, 2, :], st[:, 3, :], st[:, 2, :], ALU.max))
                link(nc.vector.reciprocal(st[:, 2, :], st[:, 2, :]))

                def head_norm(name, gate):
                    hb = sec(22).rearrange("p (g n) -> p g n", g=8)
                    link(nc.vector.tensor_reduce(st[:, 6, :], hb, AX.X, ALU.add))
                    link(ts(st[:, 6, :], st[:, 6, :], 1.0 / HD, None, ALU.mult))
                    link(tt(hb, hb, st[:, 6, :].unsqueeze(2).to_broadcast([P, 8, HD]), ALU.subtract), name + ".cen")
                    dve.wait_ge(act_done, SC.at(name + ".sq"))
                    link(nc.vector.tensor_reduce(st[:, 6, :], sec(25).rearrange("p (g n) -> p g n", g=8), AX.X, ALU.add))
                    link(ts(st[:, 0, :], st[:, 6, :], 1.0 / HD, EPS, ALU.mult, ALU.add), name + ".ms")
                    dve.wait_ge(act_done, SC.at(name + ".rstd"))
                    link(tt(hb, hb, st[:, 1, :].unsqueeze(2).to_broadcast([P, 8, HD]), ALU.mult))
                    link(tt(sec(gate), sec(gate), sec(22), ALU.mult), name + ".y")

                for t in range(NT):
                    b = quarters(filled("mly", t))
                    link(tt(tok4(22)[:, t], b, st[:, 2, 4 * t:4 * t + 4].unsqueeze(2).to_broadcast([P, H, HD]), ALU.mult),
                         ("free", "mly", t))
                dve.wait_ge(pool_done, GC.at("mloz"))
                head_norm("ml", 10)
                for t in range(NT):
                    dve.wait_ge(act_done, SC.at(f"gmv{t}"))
                    link(nc.vector.bn_stats(bst[:, 0, 0:6], tok(20)[:, t, :]))
                    link(nc.vector.bn_aggr(st[:, 7, 2 * t:2 * t + 2], bst[:, 0, 0:6]))
                for t in range(NT):
                    link(ts(st[:, 0, t:t + 1], st[:, 7, 2 * t + 1:2 * t + 2], EPS, None, ALU.add), *(["gm.ms"] if t else []))
                for h in range(H):
                    e = sbr[:, h * TRI:(h + 1) * TRI]
                    b = filled("rts", h)
                    dec = con(C_DEC + 2 * P * h, 2 * P)
                    link(tt(e[:, 0:S], b[:, 0:S], dec, ALU.mult))
                    link(tt(e[:, S:TRI], b[:, S:TRI], dec[:, 0:P], ALU.mult), f"rtsc{h}", ("free", "rts", h))
                dve.wait_ge(act_done, SC.at("gm.rstd"))
                for t in range(NT):
                    link(ts(tok(20)[:, t, :], tok(20)[:, t, :], st[:, 7, 2 * t:2 * t + 1], st[:, 1, t:t + 1], ALU.subtract, ALU.mult))
                dve.wait_ge(small2_in, (l + 1) * 48)
                for o, op in ((D, ALU.mult), (D + W, ALU.add)):
                    for t in range(NT):
                        link(tt(tok(20)[:, t, :], tok(20)[:, t, :], brow[:, o:o + W], op), *(["gmln"] if t and op == ALU.add else []))
                b = quarters(filled("wsT"))
                link(tt(wsT[:, :, :], b, con(C_GMM).unsqueeze(1).to_broadcast([P, 4, P]), ALU.mult), "wsT", ("free", "wsT", 0))
                for t in range(NT):
                    b = filled("rty", t)
                    link(nc.vector.tensor_copy(tok(22)[:, t, :], b[:, :]), ("free", "rty", t))
                dve.wait_ge(act_done, SC.at("rtz1"))
                head_norm("rt", 7)
                for h in range(H):
                    b = halves(filled("xas", h))
                    link(nc.vector.tensor_reduce(st[:, 4, 2 * h:2 * h + 2], b, AX.X, ALU.max))
                    link(ts(st[:, 4, 2 * h:2 * h + 2], st[:, 4, 2 * h:2 * h + 2], -HD ** -0.5, None, ALU.mult), f"xamax{h}")
                for t in range(NT):
                    b = filled("gmy", t)
                    for g in range(4):
                        v = tok4(19)[:, t, g, :]
                        link(stt(v, b[:, g * P:(g + 1) * P], cols[:, 48 + g:49 + g], v, ALU.add, ALU.mult),
                             *([("free", "gmy", t)] if g == 3 else []))
                dve.wait_ge(act_done, SC.at("gmz1"))
                link(tt(sec(21), sec(21), sec(19), ALU.mult), "gmy")
                dve.wait_ge(act_done, SC.at("xae3"))
                link(nc.vector.reciprocal(st[:, 5, :], st[:, 5, :]))
                mg = sec(11, 2).rearrange("p (t n) -> p t n", t=NT)

                def merge(b):
                    g = sec(8 if b % 2 == 0 else 19, 2).rearrange("p (t n) -> p t n", t=NT)
                    dve.wait_ge(act_done, SC.at(f"gate{b}"))
                    for i in range(4):
                        n, t = divmod(i, 2)
                        u = filled(f"up{b}", i)
                        gv, mv = g[:, t, n * 512:(n + 1) * 512], mg[:, t, n * 512:(n + 1) * 512]
                        if b == 0:
                            link(tt(mv, u[:, :], gv, ALU.mult), ("free", f"up{b}", i), *(["merge0"] if i == 3 else []))
                        else:
                            link(tt(gv, u[:, :], gv, ALU.mult), ("free", f"up{b}", i))
                            link(tt(mv, mv, gv, ALU.add), *([f"merge{b}"] if i == 3 else []))

                merge(0)
                merge(1)
                for t in range(NT):
                    b = filled("xay", t)
                    for h in range(H):
                        z = tok4(17)[:, t, h, :]
                        link(stt(z, b[:, h * P:(h + 1) * P], st[:, 5, 2 * h + t:2 * h + t + 1], z, ALU.mult, ALU.mult),
                             *([("free", "xay", t), f"y4{t}"] if h == 3 else []))
                for b in range(2, 5):
                    merge(b)
                mean_square("post", NT, D)
                dve.wait_ge(act_done, SC.at("post.rstd"))
                o = sec(6, 2).rearrange("p (t n) -> p t n", t=NT)
                for t in range(NT):
                    link(tt(o[:, t, :], o[:, t, :], brow[:, 0:D], ALU.mult))
                    link(stt(xs[:, t, :], o[:, t, :], st[:, 1, t:t + 1], xs[:, t, :], ALU.mult, ALU.add), *(["res"] if t else []))
                dve.sem_inc(arrived, 1)

            VC.enter("AB", True)
            dve.wait_ge(go, DEPTH + 1)
            dve.sem_inc(spare, 1)
            dve.wait_ge(mem_in, 5 * 16)
            normalise(arena[:, 0:2, :], arena[:, 2:4, :], "mem", "mem.n")
            lc = cols2[:, COL_AB + 64:COL_AB + 72]
            dve.wait_ge(act_done, SC.at("cols20"))
            link(ts(lam[:, 1, :], lc, -1.0, 0.0, ALU.mult, ALU.max))
            dve.wait_ge(act_done, SC.at("lam.ln"))
            link(tt(lam[:, 1, :], lam[:, 1, :], lam[:, 0, :], ALU.add))
            link(ts(lam[:, 2, :], lam[:, 1, :], -8.0, None, ALU.mult))
            link(ts(lam[:, 3, :], lam[:, 1, :], 8.0, None, ALU.mult), "lam")
            normalise(xs, xn, "h", "xn")
            for i in range(4):
                b = halves(filled("rec", i))
                for j in range(2):
                    ft = 2 * i + j
                    dve.wait_ge(act_done, SC.at(f"rec.tap{ft | 1}"))
                    for d in range(1, 4):
                        c = COL_AB + 8 + 8 * (3 - d) + ft
                        y = feat(2, 2)[:, ft, d:S]
                        link(stt(y, b[:, j, 0:S - d], cols2[:, c:c + 1], y, ALU.mult, ALU.add),
                             *([("free", "rec", i), f"xr{i}"] if d == 3 and j == 1 else []))
            dve.wait_ge(act_done, SC.at("gx3"))
            link(tt(sec(4, 2), sec(4, 2), sec(2, 2), ALU.mult))
            dve.wait_ge(act_done, SC.at("a"))
            link(ts(sec(10, 2), sec(8, 2), 1.0, None, ALU.add))
            link(nc.vector.reciprocal(sec(10, 2), sec(10, 2)))
            link(stt(sec(8, 2), sec(8, 2), 2.0, sec(10, 2), ALU.mult, ALU.mult), "mult2")
            dve.wait_ge(act_done, SC.at("mult"))
            link(tt(sec(4, 2), sec(4, 2), sec(8, 2), ALU.mult))
            for k in range(KD):
                link(nc.vector.tensor_tensor_scan(feat(10, 2)[:, k, :], feat(6, 2)[:, k, :], feat(4, 2)[:, k, :], 0.0,
                                                  ALU.mult, ALU.add))
            dve.wait_ge(act_done, SC.at("gate"))
            link(tt(sec(10, 2), sec(10, 2), sec(0, 2), ALU.mult), "ya")
            dve.wait_ge(act_done, SC.at("pu"))
            src = feat(12)
            for d in range(4):
                w = 2 ** d
                dst = feat(13 + d % 2)
                link(tt(dst[:, d:4, w:S], src[:, d:4, w:S], src[:, d:4, 0:S - w], ALU.add))
                link(nc.vector.tensor_copy(dst[:, d:4, 0:w], src[:, d:4, 0:w]))
                rc = con(C_RC + d * S, S)
                link(tt(feat(16)[:, d, :], dst[:, d, :], rc, ALU.mult))
                link(tt(feat(16)[:, d, :], feat(16)[:, d, :], feat(12)[:, d, :], ALU.subtract), *(["pm"] if d == 3 else []))
                src = dst
            for i in range(2):
                b = halves(filled("pl", i))
                for j in range(2):
                    g = 2 * i + j
                    link(ts(feat(15)[:, g, :], b[:, j, :], cols2[:, COL_AB + 72 + g:COL_AB + 73 + g],
                            cols2[:, COL_AB + 76 + g:COL_AB + 77 + g], ALU.add, ALU.mult),
                         *([("free", "pl", i), f"yb{i}"] if j else []))

            def residual(bias=False):
                for i in range(4):
                    n, t = divmod(i, 2)
                    b = filled("o", i)
                    xv = xs[:, t, n * 512:(n + 1) * 512]
                    link(tt(xv, b[:, :], xv, ALU.add), ("free", "o", i))
                    if bias:
                        link(tt(xv, xv, brow[:, n * 512:(n + 1) * 512], ALU.add))
                link(ts(pos_f[:, :], pos_f[:, :], 1.0, None, ALU.mult), "end", "res")

            residual()

            def cross(l):
                VC.enter(f"X{l}")
                normalise(xs, xn, "h", "xn")
                for h in range(H):
                    b = halves(filled("s", h))
                    link(nc.vector.tensor_reduce(st[:, 4, 2 * h:2 * h + 2], b, AX.X, ALU.max))
                    link(ts(st[:, 4, 2 * h:2 * h + 2], st[:, 4, 2 * h:2 * h + 2], -1.0 / 16, None, ALU.mult), f"max{h}")
                pr = sec(6, 2)
                for h in range(H):
                    dve.wait_ge(act_done, SC.at(f"e{h}"))
                    link(nc.vector.reciprocal(st[:, 5, 2 * h:2 * h + 2], st[:, 5, 2 * h:2 * h + 2]))
                    for t in range(NT):
                        v = pr[:, h * 512 + t * S:h * 512 + (t + 1) * S]
                        link(ts(v, v, st[:, 5, 2 * h + t:2 * h + t + 1], None, ALU.mult), *([f"pn{h}"] if t else []))
                residual()

            def ffn(l):
                VC.enter(f"F{l}")
                normalise(xs, xn, "h", "xn")
                w0 = COL_F[l] + 24
                for j in range(6):
                    c = feat(6 + j % 2)
                    for i in range(2):
                        b = halves(filled(f"g{j}", i))
                        for q in range(2):
                            f, ft = 2 * i + q, 4 * j + 2 * i + q
                            dve.wait_ge(act_done, SC.at(f"tap{ft | 1}"))
                            for d in range(1, 3):
                                cc = w0 + 24 * (2 - d) + ft
                                last = d == 2 and q == 1
                                link(stt(c[:, f, d:S], b[:, q, 0:S - d], cols2[:, cc:cc + 1], c[:, f, d:S], ALU.mult, ALU.add),
                                     *([("free", f"g{j}", i)] if last else []), *([f"conv{j}"] if last and i else []))
                    dve.wait_ge(act_done, SC.at(f"gelu{j}"))
                    for i in range(2):
                        b = halves(filled(f"u{j}", i))
                        link(tt(feat(j)[:, 2 * i:2 * i + 2, :], b, c[:, 2 * i:2 * i + 2, :], ALU.mult),
                             ("free", f"u{j}", i), *([f"h{j}"] if i else []))
                residual()

            cross(0)
            ffn(0)
            VC.enter("C")
            normalise(xs, xn, "h", "xn")
            for i in range(4):
                b = halves(filled("ca", i))
                dve.wait_ge(act_done, SC.at(f"cb{i}"))
                for j in range(2):
                    ft = 2 * i + j
                    link(stt(feat(2, 2)[:, ft, :], b[:, j, :], cols2[:, COL_C + 8 + ft:COL_C + 9 + ft], feat(0, 2)[:, ft, :],
                             ALU.add, ALU.mult), f"glu{ft}", *([("free", "ca", i)] if j else []))
            w0 = COL_C + 48
            for ft in range(KD):
                dve.wait_ge(act_done, SC.at(f"tap{ft}"))
                for d in range(1, 31):
                    c = w0 + 8 * (30 - d) + ft
                    y = feat(4, 2)[:, ft, d:S]
                    link(stt(y, feat(2, 2)[:, ft, 0:S - d], cols2[:, c:c + 1], y, ALU.mult, ALU.add),
                         *([f"dw{ft}"] if d == 30 else []))
            b = filled("mu", 0)
            link(ts(sec(13)[:, 0:S], b[:, 0:S], 1.0 / D, None, ALU.mult), ("free", "mu", 0))
            bc = sec(13)[:, 0:S].unsqueeze(1).to_broadcast([P, KD, S])
            link(tt(feat(6, 2), feat(4, 2), bc, ALU.subtract), "cen")
            b = filled("var", 0)
            link(ts(sec(13)[:, 0:S], b[:, 0:S], 1.0 / D, EPS, ALU.mult, ALU.add), ("free", "var", 0), "var")
            dve.wait_ge(act_done, SC.at("rstd"))
            link(tt(feat(6, 2), feat(6, 2), bc, ALU.mult), "xhat")
            residual(bias=True)
            cross(1)
            ffn(1)
            normalise(xs, sec(0, 2).rearrange("p (t d) -> p t d", t=NT), "fin", "finn")
            for t in range(NT):
                link(tt(sec(0, 2)[:, t * D:(t + 1) * D], sec(0, 2)[:, t * D:(t + 1) * D], brow[:, D:2 * D], ALU.mult),
                     *(["final"] if t else []))

        @block.tensor
        def _(pe):
            mm = nc.tensor.matmul
            loop = [None]
            used = []

            def begin(name, i=0):
                before = BEFORE[PC.stage, name, i]
                if before is not None:
                    key = ("free", *before)
                    if SC.has(key):
                        pe.wait_ge(act_done, SC.at(key))
                    elif VC.has(key):
                        pe.wait_ge(vec_done, VC.at(key))
                    else:
                        assert known is None, key
                return bank(PC, name, i)

            def end(ins, name, i=0):
                ins.then_inc(pe_done, PC((name, i)))
                give_back()

            def give_back():
                if used and used[0][1] < PC.n:
                    s, n = used.pop(0)
                    pe.wait_ge(pe_done, n)
                    pe.sem_inc(slot_free[s], 1)

            def flush():
                while used:
                    s, n = used.pop(0)
                    pe.wait_ge(pe_done, n)
                    pe.sem_inc(slot_free[s], 1)

            count = [0]

            def chunk(k, m):
                n = count[0]
                count[0] += 1
                s = n % RING
                if loop[0] is not None:
                    pe.wait_ge(slot_full[s], loop[0] * (16 * LAYER_CHUNKS // RING) + 16 * (n // RING + 1))
                else:
                    pe.wait_ge(slot_full[s], 16 * (n // RING + 1))
                return s, ring[:, s, 0:k * m].rearrange("p (k m) -> p k m", k=k)

            def spent(s):
                used.append((s, PC.n))

            def proj_T(name, w, src=hT, i0=0):
                for t in range(NT):
                    b = begin(name, i0 + t)
                    for k in range(KD):
                        ins = mm(b[:, :], src[:, k, t * P:(t + 1) * P], w[:, k, :], start=k == 0, stop=k == KD - 1)
                    end(ins, name, i0 + t)

            def proj_F(name, w, src=hT, i0=0):
                for i in range(2):
                    b = halves(begin(name, i0 + i))
                    for j in range(2):
                        c = (2 * i + j) * P
                        for k in range(KD):
                            ins = mm(b[:, j, :], w[:, k, c:c + P], src[:, k, :], start=k == 0, stop=k == KD - 1)
                    end(ins, name, i0 + i)

            def project(kind, name, src=hT, i0=0):
                s, w = chunk(KD, W)
                (proj_T if kind == "T" else proj_F)(name, w, src, i0)
                spent(s)

            def turn(name, i, src, cols_per=2):
                b = halves(begin(name, i))
                for j in range(2):
                    for t in range(NT):
                        ins = nc.tensor.transpose(b[:, j, t * P:(t + 1) * P], src[:, t, (2 * i + j) * P:(2 * i + j + 1) * P], ident)
                end(ins, name, i)

            def norm_T():
                pe.wait_ge(vec_done, VC.at("xn"))
                for i in range(4):
                    turn("hT", i, arena[:, 23:25, :])
                pe.wait_ge(act_done, SC.at("hT3"))

            PC.enter("pro")
            pe.wait_ge(const_in, 16)
            pe.wait_ge(vec_done, VC.at("mem.n"))
            for i in range(4):
                turn("memT", i, arena[:, 2:4, :])
            end(nc.tensor.transpose(ps[7][:, 0:P], ident, ident), "endpro")
            for i in range(RING):
                pe.sem_inc(slot_free[i], 1)
            pe.wait_ge(pe_done, PC.n)
            PC.marks["pro", "end"] = PC.n
            pe.sem_inc(arrived, 1)

            with pe.Fori(0, DEPTH) as l:
                loop[0] = l
                PC.enter("L", True)
                pe.wait_ge(go, l + 1)
                pe.sem_inc(spare, 1)
                pe.wait_ge(small_in, (l + 1) * (7 * 16))
                pe.sem_inc(spare, 1)
                b = begin("cols")
                end(nc.tensor.transpose(b[:, 0:52], rows[0:52, :], ident[0:52, 0:52]), "cols")
                norm_T()
                project("F", "sbq")
                project("F", "sbk")
                project("T", "sbv")
                project("T", "sbz")
                pe.wait_ge(pool_done, GC.at("mTg"))
                mTg = feat(15, 2)
                project("F", "mk", mTg)
                project("T", "mv", mTg)

                def scores(name, h, q, k):
                    b = begin(name, h)
                    mm(b[:, 0:S], k[:, h, 0:P], q[:, h, :], start=True, stop=True)
                    end(mm(b[:, S:TRI], k[:, h, P:S], q[:, h, P:S], start=False, stop=True, skip_group_check=True), name, h)

                def mix(name, t, w, v):
                    b = begin(name, t)
                    for h in range(H):
                        o = h * TRI
                        y = b[:, h * HD:(h + 1) * HD]
                        if t == 0:
                            ins = mm(y, w[:, o:o + P], v[:, 0, h * HD:(h + 1) * HD], start=True, stop=True)
                        else:
                            mm(y, w[:, o + P:o + S], v[:, 0, h * HD:(h + 1) * HD], start=True, stop=False)
                            ins = mm(y, w[:, o + S:o + TRI], v[:, 1, h * HD:(h + 1) * HD], start=False, stop=True)
                    end(ins, name, t)

                for h in range(H):
                    scores("sbs", h, feat(0), feat(1))
                project("F", "mlq")
                project("F", "mlk")
                sbr = sec(13, 2)
                for h in range(H):
                    pe.wait_ge(vec_done, VC.at(f"sblk{h}"))
                    b = bank(PC, "sbw", h)
                    e = sbr[:, h * TRI:(h + 1) * TRI]
                    mm(b[:, 0:S], con(C_TRI), e[:, 0:S], start=False, stop=False, skip_group_check=True)
                    mm(b[:, P:S], ones, e[:, S:TRI], start=False, stop=False, skip_group_check=True)
                    end(mm(b[:, S:TRI], con(C_TRI), e[:, S:TRI], start=False, stop=True, skip_group_check=True), "sbw", h)
                project("T", "mlv")
                project("T", "mlo")
                project("T", "mlz")
                s, w = chunk(KD, 2 * H)
                b = begin("mlif")
                for n in range(2):
                    for k in range(KD):
                        ins = mm(b[0:H, n * S:(n + 1) * S], w[:, k, n * H:(n + 1) * H], hT[:, k, :], start=k == 0, stop=k == KD - 1)
                end(ins, "mlif")
                spent(s)
                pe.wait_ge(act_done, SC.at("sbw3"))
                for t in range(NT):
                    mix("sby", t, sbr, tok(2))
                for kind, name in ("T", "rtq"), ("T", "rtk"), ("T", "rtv"), ("T", "rtz"):
                    project(kind, name)
                pe.wait_ge(vec_done, VC.at("mlrows"))
                b = begin("mle")
                for n, r in enumerate((7, 4)):
                    for t in range(NT):
                        c = 8 * n + 4 * t
                        ins = nc.tensor.transpose(b[:, c:c + H], gr[0:H, r, t * P:(t + 1) * P], ident[0:H, 0:H])
                end(ins, "mle")
                for h in range(H):
                    b = begin("mld", h)
                    sel = cst[0:H, C_SEL + h * P:C_SEL + (h + 1) * P]
                    mm(b[:, 0:S], sel, gr[0:H, 6, :], start=True, stop=False)
                    mm(b[:, 0:P], ident, con(C_MLN), start=False, stop=True)
                    mm(b[:, S:TRI], sel, gr[0:H, 6, P:S], start=True, stop=False)
                    end(mm(b[:, S:TRI], ident, con(C_MLN), start=False, stop=True), "mld", h)
                pe.wait_ge(act_done, SC.at("mlk"))
                for h in range(H):
                    scores("mls", h, feat(11), feat(12))
                project("T", "gmu")
                project("T", "gmv")
                pe.wait_ge(vec_done, VC.at("mlsc3"))
                mlr = sec(15, 2)
                b = begin("mln")
                for h in range(H):
                    o = h * TRI
                    mm(b[:, h:h + 1], mlr[:, o:o + P], ones[:, 0:1], start=True, stop=True)
                    mm(b[:, H + h:H + h + 1], mlr[:, o + P:o + S], ones[:, 0:1], start=True, stop=False)
                    ins = mm(b[:, H + h:H + h + 1], mlr[:, o + S:o + TRI], ones[:, 0:1], start=False, stop=True)
                end(ins, "mln")
                for t in range(NT):
                    mix("mly", t, mlr, tok(8))
                project("T", "gmz")
                for name, s_ in (("rtq", 17), ("rtk", 18)):
                    pe.wait_ge(vec_done, VC.at(name + "r"))
                    for i in range(2):
                        turn({"rtq": "rqT", "rtk": "rkT"}[name], i, tok(s_))
                pe.wait_ge(act_done, SC.at("rkT1"))
                for h in range(H):
                    scores("rts", h, feat(0), feat(1))
                s, w = chunk(4, P)
                b = quarters(begin("wsT"))
                for g in range(4):
                    ins = nc.tensor.transpose(b[:, g, :], w[:, g, :], ident)
                end(ins, "wsT")
                spent(s)
                project("F", "xaq")
                project("T", "xaz")
                pe.wait_ge(vec_done, VC.at("rtsc3"))
                for t in range(NT):
                    mix("rty", t, sbr, tok(6))
                pe.wait_ge(act_done, SC.at("xaq1"))
                for h in range(H):
                    b = halves(begin("xas", h))
                    for t in range(NT):
                        ins = mm(b[:, t, :], feat(2)[:, h, t * P:(t + 1) * P], feat(4)[:, h, :], start=True, stop=True)
                    end(ins, "xas", h)
                pe.wait_ge(vec_done, VC.at("gmln"))
                for t in range(NT):
                    b = quarters(begin("gmy", t))
                    for g in range(4):
                        ins = mm(b[:, g, :], wsT[:, g, :], tok4(20)[:, t, g, :], start=True, stop=True)
                    end(ins, "gmy", t)

                YS = [3, 10, 21, 7, 17]

                def gates(b_, ready):
                    project("T", f"gate{b_}", i0=0)
                    project("T", f"gate{b_}", i0=2)
                    pe.wait_ge(vec_done, VC.at(ready))
                    for i in range(2):
                        turn(f"yT{b_}", i, tok(YS[b_]))
                    s, w = chunk(4, D)
                    pe.wait_ge(act_done, SC.at(f"yT{b_}"))
                    y = feat(23 + b_ % 2)
                    for i in range(4):
                        n, t = divmod(i, 2)
                        bk = begin(f"up{b_}", i)
                        for k in range(4):
                            ins = mm(bk[:, :], y[:, k, t * P:(t + 1) * P], w[:, k, n * 512:(n + 1) * 512], start=k == 0, stop=k == 3)
                        end(ins, f"up{b_}", i)
                    spent(s)

                gates(0, "y01")
                for h in range(H):
                    pe.wait_ge(act_done, SC.at(f"xae{h}"))
                    b = halves(begin("xap", h))
                    for m in range(2):
                        for t in range(NT):
                            o = h * 512 + t * S + m * P
                            ins = nc.tensor.transpose(b[:, m, t * P:(t + 1) * P], sec(15, 2)[:, o:o + P], ident)
                    end(ins, "xap", h)
                gates(1, "ml.y")
                pe.wait_ge(act_done, SC.at("xap3"))
                for t in range(NT):
                    b = begin("xay", t)
                    for h in range(H):
                        for m in range(2):
                            o = h * 512 + m * S + t * P
                            ins = mm(b[:, h * HD:(h + 1) * HD], sec(13, 2)[:, o:o + P], tok(5)[:, m, h * HD:(h + 1) * HD],
                                     start=m == 0, stop=m == 1)
                    end(ins, "xay", t)
                gates(2, "gmy")
                gates(3, "rt.y")
                gates(4, "y41")
                pe.wait_ge(vec_done, VC.at("merge4"))
                for i in range(4):
                    turn("mgT", i, sec(11, 2).rearrange("p (t n) -> p t n", t=NT))
                pe.wait_ge(act_done, SC.at("mgT"))
                for n in range(2):
                    project("T", "o", feat(0, 2), i0=2 * n)
                flush()
                pe.wait_ge(pe_done, PC.n)
                pe.sem_inc(arrived, 1)

            loop[0] = None
            assert count[0] == LAYER_CHUNKS
            count[0] = DEPTH * LAYER_CHUNKS

            def finish():
                PC.marks[PC.stage, "end"] = PC.n

            PC.enter("AB", True)
            pe.wait_ge(go, DEPTH + 1)
            pe.sem_inc(spare, 1)
            pe.wait_ge(rows2_in, ROWS2)
            for i, tiles in enumerate(([(0, 80, 0), (1, 48, COL_C), (2, 124, COL_C + 48), (3, 124, COL_C + 172), (4, 120, COL_F[0])],
                                       [(5, 120, 0)])):
                b = begin("cols2", i)
                for t_, n, c in tiles:
                    ins = nc.tensor.transpose(b[:, c:c + n], arena[0:n, 20, t_ * P:(t_ + 1) * P], ident[0:n, 0:n])
                end(ins, "cols2", i)
            pe.wait_ge(vec_done, VC.at("mem.n"))
            for i in range(4):
                turn("memT", i, arena[:, 2:4, :])
            norm_T()
            project("F", "rec", i0=0)
            project("F", "rec", i0=2)
            for name in ("ga", "gx"):
                s, w = chunk(8, P)
                for i in range(4):
                    pe.wait_ge(vec_done, VC.at(f"xr{i}"))
                    b = halves(begin(name, i))
                    for j in range(2):
                        ins = mm(b[:, j, :], w[:, 2 * i + j, :], feat(2, 2)[:, 2 * i + j, :], start=True, stop=True)
                    end(ins, name, i)
                spent(s)
            project("F", "gate", i0=0)
            project("F", "gate", i0=2)
            project("F", "pu")
            s, w = chunk(4, P)
            pe.wait_ge(vec_done, VC.at("pm"))
            for i in range(2):
                b = halves(begin("pl", i))
                for j in range(2):
                    ins = mm(b[:, j, :], w[:, 2 * i + j, :], feat(16)[:, 2 * i + j, :], start=True, stop=True)
                end(ins, "pl", i)
            spent(s)
            pe.wait_ge(vec_done, VC.at("yb1"))

            def down(j, n_chunks, src):
                s, w = chunk(4, D)
                for i in range(4):
                    n, t = divmod(i, 2)
                    b = begin("o", i) if j == 0 else bank(PC, "o", i)
                    for k in range(4):
                        ins = mm(b[:, :], src[:, k, t * P:(t + 1) * P], w[:, k, n * 512:(n + 1) * 512],
                                 start=j == 0 and k == 0, stop=j == n_chunks - 1 and k == 3)
                    if j == n_chunks - 1:
                        end(ins, "o", i)
                    else:
                        ins.then_inc(pe_done, PC())
                        give_back()
                spent(s)

            for j, src in enumerate((feat(10), feat(11), feat(15))):
                down(j, 3, src)
            finish()

            def cross(l):
                PC.enter(f"X{l}")
                norm_T()
                project("F", "q", i0=0)
                project("F", "q", i0=2)
                pe.wait_ge(pool_done, GC.at("mTg"))
                for kind, name in ("F", "k"), ("T", "v"):
                    for i0 in (0, 2):
                        project(kind, name, feat(12, 2), i0)
                q, k = feat(0, 2), feat(2, 2)
                pe.wait_ge(act_done, SC.at("k"))
                for h in range(H):
                    b = halves(begin("s", h))
                    for t in range(NT):
                        for d in range(2):
                            ins = mm(b[:, t, :], q[:, 2 * h + d, t * P:(t + 1) * P], k[:, 2 * h + d, :], start=d == 0, stop=d == 1)
                    end(ins, "s", h)
                for h in range(H):
                    pe.wait_ge(vec_done, VC.at(f"pn{h}"))
                    b = halves(begin("p", h))
                    for m in range(2):
                        for t in range(NT):
                            o = h * 512 + t * S + m * P
                            ins = nc.tensor.transpose(b[:, m, t * P:(t + 1) * P], sec(6, 2)[:, o:o + P], ident)
                    end(ins, "p", h)
                v = sec(4, 2).rearrange("p (t n) -> p t n", t=NT)
                for h in range(H):
                    pe.wait_ge(act_done, SC.at(f"pT{h}"))
                    b = halves(begin("oT", h))
                    for d in range(2):
                        for m in range(2):
                            c = h * 256 + d * P
                            ins = mm(b[:, d, :], v[:, m, c:c + P], sec(8, 2)[:, h * 512 + m * S:h * 512 + (m + 1) * S],
                                     start=m == 0, stop=m == 1)
                    end(ins, "oT", h)
                pe.wait_ge(act_done, SC.at("oT"))
                for n in range(2):
                    project("T", "o", feat(10, 2), i0=2 * n)
                finish()

            def ffn(l):
                PC.enter(f"F{l}")
                norm_T()
                for j in range(6):
                    project("F", f"g{j}")
                    project("F", f"u{j}")
                    if j:
                        pe.wait_ge(vec_done, VC.at(f"h{j - 1}"))
                        down(j - 1, 6, feat(j - 1))
                pe.wait_ge(vec_done, VC.at("h5"))
                down(5, 6, feat(5))
                finish()

            cross(0)
            ffn(0)
            PC.enter("C")
            norm_T()
            for name in ("cb", "ca"):
                for i0 in (0, 2):
                    project("F", name, i0=i0)
            b = begin("mu", 0)
            for k in range(KD):
                pe.wait_ge(vec_done, VC.at(f"dw{k}"))
                ins = mm(b[:, 0:S], ones, feat(4, 2)[:, k, :], start=k == 0, stop=k == KD - 1)
            end(ins, "mu", 0)
            pe.wait_ge(act_done, SC.at("sq"))
            b = begin("var", 0)
            for k in range(KD):
                ins = mm(b[:, 0:S], ones, feat(8, 2)[:, k, :], start=k == 0, stop=k == KD - 1)
            end(ins, "var", 0)
            pe.wait_ge(act_done, SC.at("silu"))
            for n in range(2):
                project("T", "o", feat(10, 2), i0=2 * n)
            finish()
            cross(1)
            ffn(1)
            flush()

    return [C.marks for C in (PC, SC, VC, GC)]


COL_AB, COL_C, COL_F = 0, 80, (376, 496)
ROWS2 = 25 * 16

_INS = ["x", "mem", "positions", "norm_pre", "norm_post", "w_in", "b_igate", "b_fgate", "conv_q", "conv_k", "gm_ln_g",
        "gm_ln_b", "gm_ws", "gm_bs", "mem_norm", "w_mem_kv", "w_up", "w_out", "mem_2", "ab_norm_2", "ab_w_in_2",
        "a_conv_w_2", "a_conv_b_2", "a_gate_x_w_2", "a_gate_x_b_2", "a_gate_a_w_2", "a_gate_a_b_2", "a_lambda_2",
        "b_group_w_2", "b_group_b_2", "b_scale_2", "ab_w_out_2", "c_norm_2", "c_w_pw1_2", "c_b_pw1_2", "c_dw_w_2",
        "c_dw_b_2", "c_ln_g_2", "c_ln_b_2", "c_w_pw2_2", "c_b_pw2_2", "xa_norm_2", "xa_mem_norm_2", "xa_wq_2",
        "xa_wk_2", "xa_wv_2", "xa_wo_2", "f_norm_2", "f_w_up_2", "f_dw_w_2", "f_dw_b_2", "f_w_down_2", "final_norm_2"]


def kernel(**inputs):
    import numpy as _np
    import concourse.bacc as _bacc
    from concourse import mybir as _mybir
    from concourse.bass_utils import run_bass_kernel_spmd as _run

    arrays = {f"in_{n}_dram": _np.ascontiguousarray(inputs[n]) for n in _INS}
    arrays["in_constants_dram"] = constants()
    known = None
    for _ in range(2):
        nc = _bacc.Bacc("TRN2", target_bir_lowering=False, num_devices=1)
        A = {n: nc.dram_tensor(f"in_{n}_dram", arrays[f"in_{n}_dram"].shape,
                               _mybir.dt.from_np(arrays[f"in_{n}_dram"].dtype), kind="ExternalInput").ap()
             for n in _INS + ["constants"]}
        out = nc.dram_tensor("out_0_dram", (1, S, D), F32, kind="ExternalOutput").ap()
        known = build(nc, A, out, known)
    r = _run(nc, [arrays], core_ids=[0])
    return r.results[0]["out_0_dram"]
```

```python
import concourse.bass as bass
import numpy as np
from concourse import mybir
from contextlib import ExitStack

F32 = mybir.dt.float32
F32R = mybir.dt.float32r
I32 = mybir.dt.int32
ACT = mybir.ActivationFunctionType
ALU = mybir.AluOpType
AX = mybir.AxisListType

P = 128
S, D = 256, 1024
NT, KD = S // P, D // P
DEPTH = 2
W = D // 2
H, HD = 4, P
EPS = 1e-6
BIG = 1e30
RAW = 5
SPLIT = 4
AHEAD = 3
BANKS = 8
FF = 3 * D
KF = FF // P
TRI = 3 * P

SBQ, SBK, SBV, SBZ = (i * W for i in range(4))
MLQ, MLK, MLV, MLO, MLZ = (4 * W + i * W for i in range(5))
MLI = 9 * W
MLF = MLI + H
GMU, GMV, GMZ = (MLF + H + i * W for i in range(3))
RTQ, RTK, RTV, RTZ = (GMZ + W + i * W for i in range(4))
XAQ, XAZ = RTZ + W, RTZ + 2 * W
GATE = XAZ + W

C_ID, C_TRI, C_LKM, C_NB, C_MLN, C_GMM = 0, 128, 256, 640, 1024, 1152
C_DEC, C_INV, C_ONE = 1280, 2304, 2368
C_ALL = 2496


def constants():
    c = np.zeros((P, C_ALL), np.float32)
    i, j = np.arange(P)[:, None], np.arange(P)[None, :]
    c[:, C_ID:C_ID + P] = i == j
    c[:, C_TRI:C_TRI + P] = i >= j
    for at, inner, valid, other in ((C_LKM, -1.0, 0.0, -1.0), (C_NB, 0.0, -BIG, 0.0)):
        for o in (0, 2 * P):
            c[:, at + o:at + o + P] = np.where(i < j, inner, valid)
        c[:, at + P:at + 2 * P] = other
    c[:, C_MLN:C_MLN + P] = np.where(i <= j, 0.0, -BIG)
    c[:, C_GMM:C_GMM + P] = i // 64 <= j // 64
    gamma = np.log(1.0 - 2.0 ** (-5.0 - np.arange(H)))
    for h in range(H):
        at = C_DEC + 2 * P * h
        c[:, at:at + P] = np.where(i // 64 <= j // 64, np.exp(gamma[h] * np.abs(i - j)), 0) * HD ** -0.5
        c[:, at + P:at + 2 * P] = np.exp(gamma[h] * (j + P - i)) * HD ** -0.5
    c[:, C_INV:C_INV + 64] = np.float32(10000.0) ** (-np.arange(64, dtype=np.float32) / np.float32(64))
    c[:, C_ONE:C_ONE + P] = 1.0
    return c


def windows():
    t = np.arange(1, S + 1)
    return np.tile(np.concatenate([1.0 / np.minimum(t, 2 ** (g + 1)) for g in range(4)]).astype(np.float32), (P, 1))


class Count:

    def __init__(self, known, now):
        self.known, self.marks, self.n, self.now = known, {}, 0, now
        self.split = 0
        self.unit = 0

    @property
    def stage(self):
        return self.now[0]

    def enter(self, stage, restart=False):
        self.now[0] = stage
        if restart:
            self.n = 0

    def __call__(self, *names):
        self.n += 1
        for name in names:
            assert (self.stage, name) not in self.marks, name
            self.marks[self.stage, name] = self.n
            self.marks["split", self.stage, name] = self.split
            self.marks["unit", self.stage, name] = self.unit
        return 1

    def split_at(self, name, stage=None):
        return self.known["split", stage or self.stage, name] if self.known else 0

    def unit_at(self, name):
        return self.known["unit", self.stage, name] if self.known else 0

    def at(self, name, stage=None):
        if self.known is None:
            return 1
        return self.known[stage or self.stage, name]

    def has(self, name):
        return self.known is not None and (self.stage, name) in self.known


def build(nc, A, out, known):
    kn = known or [None] * 4
    now = [None]
    PC, SC, VC, GC = (Count(kn[i], now) for i in range(4))
    ctx = ExitStack()
    with ctx:
        def sb(name, shape, dt=F32):
            return ctx.enter_context(nc.sbuf_tensor(name, shape, dt))

        def sem(name):
            return ctx.enter_context(nc.semaphore(name))

        xs = sb("x_tokens", [P, NT, D])
        h_hi = sb("h_hi", [P, KD, S], F32R)
        h_lo = sb("h_lo", [P, KD, S], F32R)
        memT = sb("mem_features", [P, KD, S])
        raw = sb("weights_raw", [P, RAW, 1024])
        w_hi = sb("weights_hi", [P, SPLIT, 1024], F32R)
        w_lo = sb("weights_lo", [P, SPLIT, 1024], F32R)
        arena = sb("arena", [P, 24, 1024])
        cst = sb("constants_sb", [P, C_ALL])
        wsT = sb("spatial_weights", [P, 4, P])
        rows = sb("vector_rows", [P, P])
        rows2 = sb("vector_rows_2", [P, 6 * P])
        cols = sb("vector_columns", [P, 52])
        cols2 = sb("vector_columns_2", [P, 616])
        brow = sb("row_vectors", [P, 2048])
        trig = sb("cos_sin", [P, 2, NT, 64])
        pos_i = sb("positions_int", [P, NT], I32)
        pos_f = sb("positions_float", [P, NT])
        bif = sb("gate_biases", [H, 2])
        gr = arena[0:H, 23, :].rearrange("p (r s) -> p r s", s=S)
        st = sb("statistics", [P, 16, 8])
        ifc = sb("gate_columns", [P, 2, 2 * H])
        bst = sb("bn_statistics", [P, 2, 8])
        lam = sb("lambda_columns", [P, 4, 8])
        epsc = sb("eps_column", [P, 1])
        ps = [ctx.enter_context(nc.psum_tensor(f"bank{i}", [P, 512], F32)) for i in range(BANKS)]

        pe_done, act_done, vec_done, pool_done = (sem(n) for n in ("pe_done", "act_done", "vec_done", "pool_done"))
        raw_full = [sem(f"raw{i}_full") for i in range(RAW)]
        raw_free = [sem(f"raw{i}_free") for i in range(RAW)]
        hi_done = [sem(f"split{i}_hi_done") for i in range(SPLIT)]
        split_full = [sem(f"split{i}_full") for i in range(SPLIT)]
        split_free = [sem(f"split{i}_free") for i in range(SPLIT)]
        const_in, x_in, mem_in, small_in = sem("const_in"), sem("x_in"), sem("mem_in"), sem("small_in")
        small2_in, rows2_in, out_done = sem("small2_in"), sem("rows2_in"), sem("out_done")
        rows_in, mem2_in = sem("rows_in"), sem("mem2_in")
        arrived, go, spare = sem("layer_arrived"), sem("layer_go"), sem("spare")

        def sec(i, n=1):
            return arena[:, i:i + n, :].rearrange("p a n -> p (a n)")

        def tok(i):
            return arena[:, i, :].rearrange("p (t n) -> p t n", t=NT)

        def tok4(i):
            return arena[:, i, :].rearrange("p (t h n) -> p t h n", t=NT, h=H)

        def feat(i, n=1):
            return sec(i, n).rearrange("p (j s) -> p j s", s=S)

        def con(at, n=P):
            return cst[:, at:at + n]

        ident, ones = con(C_ID), con(C_ONE)

        def two(*names):
            return [(n, i) for n in names for i in range(2)]

        def four(*names):
            return [(n, i) for n in names for i in range(4)]

        GATES = lambda b: two(f"yT{b}") + four(f"gate{b}", f"up{b}")
        ORDER = {
            "pro": four("memT"),
            "L": ([("cols", 0)] + four("hT") + two("sbq", "sbk", "sbv", "sbz", "mk", "mv") + four("sbs")
                  + two("mlq", "mlk") + four("sbw") + two("mlv", "mlo", "mlz") + [("mlif", 0)]
                  + two("sby") + [("mlifT", 0)] + two( "rtq", "rtk", "rtv", "rtz") + [("mle", 0)] + four("mld", "mls")
                  + two("gmu", "gmv") + [("mln", 0)] + two("mly", "gmz") + two("rqT", "rkT") + four("rts")
                  + [("wsT", 0)] + two("xaq", "xaz", "rty") + four("xas") + two("gmy")
                  + GATES(0) + four("xap") + GATES(1) + two("xay") + GATES(2) + GATES(3) + GATES(4)
                  + four("mgT", "o")),
            "AB": ([("cols2", i) for i in range(2)] + four("hT", "rec", "memT", "ga", "gx", "gate")
                   + two("pu", "pl") + four("o")),
            "C": four("hT", "cb", "ca", "k", "v") + two("mu", "var") + four("o"),
        }
        for s in range(DEPTH):
            ORDER[f"X{s}"] = (four("k", "v") if s == 0 else []) + four("hT", "q", "s", "p", "oT", "o")
            ORDER[f"F{s}"] = (four("hT") + [("o", i) for i in range(4)]
                              + [g for j in range(6) for g in two(f"g{j}", f"u{j}")])
        HELD = {"sbw": "sbs"}

        PLACE, BEFORE = {}, {}
        for stage, order in ORDER.items():
            last = {}
            g = 0
            for name, i in order:
                if name in HELD:
                    PLACE[stage, name, i] = PLACE[stage, HELD[name], i]
                    last[PLACE[stage, name, i]] = (name, i)
                    continue
                if stage[0] == "F" and name != "hT":
                    b = 4 + i if name == "o" else g % 4
                else:
                    b = g % BANKS
                PLACE[stage, name, i] = b
                BEFORE[stage, name, i] = last.get(b)
                last[b] = (name, i)
                g += 1

        def bank(C, name, i=0):
            return ps[PLACE[C.stage, name, i]]

        def halves(b):
            return b[:, :].rearrange("p (j s) -> p j s", j=2)

        def quarters(b):
            return b[:, :].rearrange("p (h n) -> p h n", h=4)

        def kmaj(ap):
            return ap.rearrange("(k p) n -> p k n", p=P)

        def pairs(ap):
            return [ap[:, 2 * u:2 * u + 2, :] for u in range(KD // 2)]

        def singles(ap):
            return [ap[:, u:u + 1, :] for u in range(4)]

        def half(ap, c):
            return ap[:, :, c * W:(c + 1) * W]

        def layer_units(l):
            win, wm, out_w = kmaj(A["w_in"][l]), kmaj(A["w_mem_kv"][l]), kmaj(A["w_out"][l])
            got = []

            def add(split, units):
                got.extend((split, u) for u in units)

            def h(*at):
                for c in at:
                    add(True, pairs(win[:, :, c:c + W]))

            h(SBQ, SBK, SBV, SBZ)
            add(False, pairs(half(wm, 0)) + pairs(half(wm, 1)))
            h(MLQ, MLK, MLV, MLO, MLZ)
            add(False, [win[:, :, MLI:MLI + 2 * H]])
            h(RTQ, RTK, RTV, RTZ, GMU, GMV, GMZ)
            add(False, [A["gm_ws"][l].rearrange("g p q -> p g q")])
            h(XAQ, XAZ)
            for b in range(5):
                h(GATE + b * D, GATE + b * D + W)
                add(False, singles(kmaj(A["w_up"][l, b])))
            add(False, pairs(half(out_w, 0)) + pairs(half(out_w, 1)))
            return got

        def rest_units():
            got = []

            def add(split, units):
                got.extend((split, u) for u in units)

            def square(split, name, l, *cols):
                for c in cols:
                    add(split, pairs(half(kmaj(A[name][l]), c)))

            def memory_units(l):
                for name in ("xa_wk_2", "xa_wv_2"):
                    square(False, name, l, 0, 1)

            def cross_units(l):
                square(True, "xa_wq_2", l, 0, 1)
                square(False, "xa_wo_2", l, 0, 1)

            def ffn_units(l):
                dn = kmaj(A["f_w_down_2"][l])
                for j in range(7):
                    if j < 6:
                        square(True, "f_w_up_2", l, j, 6 + j)
                    if j:
                        add(False, singles(dn[:, 4 * j - 4:4 * j, :]))

            def head_weights(name):
                return A[name][0].rearrange("h i j -> i h j")

            square(True, "ab_w_in_2", 0, 2, 3)
            add(False, [head_weights("a_gate_a_w_2"), head_weights("a_gate_x_w_2")])
            square(True, "ab_w_in_2", 0, 0, 1, 4)
            add(False, [head_weights("b_group_w_2")])
            for j in range(3):
                add(False, singles(kmaj(A["ab_w_out_2"][0])[:, 4 * j:4 * j + 4, :]))
            memory_units(0)
            cross_units(0)
            ffn_units(0)
            square(True, "c_w_pw1_2", 0, 2, 3, 0, 1)
            memory_units(1)
            square(False, "c_w_pw2_2", 0, 0, 1)
            cross_units(1)
            ffn_units(1)
            return got

        KINDS = [sp_ for sp_, _ in layer_units(0)]
        REST = rest_units()
        LAYER_UNITS, LAYER_SPLIT = len(KINDS), sum(KINDS)
        assert LAYER_UNITS % RAW == 0 and LAYER_SPLIT % SPLIT == 0 and not any(KINDS[-RAW:])
        PLAIN = [sum(not k for k in KINDS[i_::RAW]) for i_ in range(RAW)]

        def unit_plan(kinds, n0, q0, plain0, before0):
            plan, q, plain, before = [], q0, list(plain0), list(before0)
            for n, k in enumerate(kinds, n0):
                r = n % RAW
                plan.append((r, n // RAW + 1, q if k else None, before[r]))
                if k:
                    before[r] = ("split", q)
                    q += 1
                else:
                    plain[r] += 1
                    before[r] = ("plain", plain[r])
            return plan

        LPLAN = unit_plan(KINDS, 0, 0, [0] * RAW, [("plain", 0)] * RAW)
        RPLAN = unit_plan([k for k, _ in REST], DEPTH * LAYER_UNITS, DEPTH * LAYER_SPLIT, [DEPTH * p_ for p_ in PLAIN],
                          [("plain", DEPTH * p_) for p_ in PLAIN])

        class Units:

            def __init__(self):
                self.l, self.plan = None, RPLAN

            def enter(self, l, plan):
                self.l, self.plan = l, plan
                self.splits = [u for u in plan if u[2] is not None]

            def count(self, per_layer, n):
                return n if self.l is None else self.l * per_layer + n

        def splitter(eng, C, units, emit):
            def up_to(n, ahead=0, unit=0):
                while n < len(units.splits) and ahead and units.plan.index(units.splits[n]) < unit + RAW - 1:
                    n, ahead = n + 1, ahead - 1
                while C.split < n:
                    emit(*units.splits[C.split])
                    C.split += 1
            return up_to

        block = ctx.enter_context(nc.Block())

        @block.sync
        def _(sp):
            sp.dma_start(cst[:, :], A["constants"]).then_inc(const_in, 16)
            sp.dma_start(xs[:, :, :], A["x"][0].rearrange("(t p) d -> p t d", p=P)).then_inc(x_in, 16)

            def load(src, r, l, before):
                kind, n = before
                if kind == "plain":
                    sp.wait_ge(raw_free[r], n + 1 if l is None else l * PLAIN[r] + n + 1)
                else:
                    sp.wait_ge(split_full[n % SPLIT], n // SPLIT + 1 if l is None else l * (LAYER_SPLIT // SPLIT) + n // SPLIT + 1)
                if l is not None:
                    sp.sem_inc(spare, 1)
                k, m = src.shape[1], src.shape[2]
                dst = raw[:, r, 0:k * m].rearrange("p (k m) -> p k m", k=k)
                if m < 64:
                    with nc.allow_non_contiguous_dma(reason="eight gate columns"):
                        sp.dma_start(dst, src).then_inc(raw_full[r], 16)
                else:
                    sp.dma_start(dst, src).then_inc(raw_full[r], 16)

            with sp.Fori(0, DEPTH) as l:
                for (_, src), (r, _, _, before) in zip(layer_units(l), LPLAN):
                    load(src, r, l, before)
            for (_, src), (r, _, _, before) in zip(REST, RPLAN):
                load(src, r, None, before)
            sp.wait_ge(vec_done, VC.at("final", "F1") if known else 1)
            sp.dma_start(out[0].rearrange("(t p) d -> p t d", p=P),
                         sec(0, 2).rearrange("p (t d) -> p t d", t=NT)).then_inc(out_done, 16)
            sp.wait_ge(out_done, 16)

        @block.gpsimd
        def _(pool):
            GC.enter("pro")

            def link(ins, *names):
                ins.then_inc(pool_done, GC(*names))
                pool.wait_ge(pool_done, GC.n)

            def mem_gain(col, dst, c):
                for k in range(KD):
                    ins = nc.gpsimd.tensor_scalar(dst[:, k, :], memT[:, k, :], c[:, col + k:col + k + 1], None, ALU.mult)
                ins.then_inc(pool_done, GC("mTg"))

            nc.gpsimd.memset(epsc[:, :], EPS).then_inc(pool_done, GC("eps"))
            r128 = "(r c) -> r c"

            def load_rows(l):
                for src, r0, n in ((A["norm_pre"][l].rearrange(r128, c=P), 0, 8),
                                   (A["mem_norm"][l].rearrange(r128, c=P), 8, 8),
                                   (A["conv_q"][l].rearrange("k (r c) -> (k r) c", c=P), 16, 16),
                                   (A["conv_k"][l].rearrange("k (r c) -> (k r) c", c=P), 32, 16),
                                   (A["gm_bs"][l], 48, 4)):
                    pool.dma_start(rows[r0:r0 + n, :], src).then_inc(rows_in, 16)

            pool.dma_start(arena[:, 0:2, :], A["mem"][0].rearrange("(t p) d -> p t d", p=P)).then_inc(mem_in, 16)
            with nc.allow_non_contiguous_dma(reason="one position per partition"):
                pool.dma_start(pos_i[:, :], A["positions"][0].rearrange("(t p) -> p t", p=P)).then_inc(mem_in, 16)
            load_rows(0)
            R = lambda t: rows2[:, t * P:(t + 1) * P]
            todo = []
            def put(t, r, ap):
                todo.append((R(t)[r:r + ap.shape[0], :], ap))
            at = 0
            for name in ("ab_norm_2", "a_conv_w_2", "a_conv_b_2", "a_gate_x_b_2", "a_gate_a_b_2", "a_lambda_2",
                         "b_group_b_2", "b_scale_2"):
                ap = A[name][0]
                ap = ap.rearrange("k (r c) -> (k r) c", c=P) if len(ap.shape) == 2 else ap.rearrange(r128, c=P)
                put(0, at, ap)
                at += ap.shape[0]
            assert at == 80
            at = 0
            for name in ("c_norm_2", "c_b_pw1_2", "c_dw_b_2", "c_ln_g_2", "c_ln_b_2"):
                ap = A[name][0].rearrange(r128, c=P)
                put(1, at, ap)
                at += ap.shape[0]
            dw = A["c_dw_w_2"][0].rearrange("k (r c) -> (k r) c", c=P)
            put(2, 0, dw[0:124, :])
            put(3, 0, dw[124:248, :])
            for l in range(DEPTH):
                at = 0
                for name in ("xa_norm_2", "xa_mem_norm_2", "f_norm_2", "f_dw_w_2", "f_dw_b_2"):
                    ap = A[name][l]
                    ap = ap.rearrange("k (r c) -> (k r) c", c=P) if len(ap.shape) == 2 else ap.rearrange(r128, c=P)
                    put(4 + l, at, ap)
                    at += ap.shape[0]
                assert at == 120
            for dst, src in todo:
                pool.dma_start(dst, src).then_inc(rows2_in, 16)
            assert len(todo) * 16 == ROWS2
            with pool.Fori(0, DEPTH) as l:
                GC.enter("L", True)
                pool.wait_ge(go, l + 1)
                pool.sem_inc(spare, 1)
                for n, name in enumerate(("b_igate", "b_fgate")):
                    with nc.allow_non_contiguous_dma(reason="one bias per partition"):
                        pool.dma_start(bif[:, n:n + 1], A[name][l].rearrange("(h a) -> h a", a=1)).then_inc(small_in, 16)
                for name, o, n in (("norm_post", 0, D), ("gm_ln_g", D, W), ("gm_ln_b", D + W, W)):
                    pool.dma_start(brow[:, o:o + n], A[name][l].rearrange("(a n) -> a n", a=1).to_broadcast([P, n])).then_inc(small2_in, 16)
                pool.wait_ge(act_done, SC.at("cols"))
                load_rows(DEPTH - 1)
                mem_gain(8, feat(15, 2), cols)
                pool.wait_ge(act_done, SC.at("mlz"))
                nc.gpsimd.tensor_tensor(sec(10), sec(10), sec(9), ALU.mult).then_inc(pool_done, GC("mloz"))
                pool.wait_ge(pool_done, GC.n)
                pool.sem_inc(arrived, 1)
                pool.wait_ge(arrived, (l + 1) * 4)
                pool.sem_inc(spare, 1)
                for s in (pe_done, act_done, vec_done, pool_done):
                    pool.sem_clear(s)
                pool.sem_inc(go, 1)
            GC.enter("AB", True)
            pool.wait_ge(go, DEPTH + 1)
            pool.sem_inc(spare, 1)
            pool.dma_start(arena[:, 18:20, :], A["mem_2"][0].rearrange("(t p) d -> p t d", p=P)).then_inc(mem2_in, 16)
            pool.dma_start(brow[:, 0:D], A["c_b_pw2_2"].to_broadcast([P, D])).then_inc(mem_in, 16)
            pool.dma_start(brow[:, D:2 * D], A["final_norm_2"].rearrange("(a d) -> a d", a=1).to_broadcast([P, D]))\
                .then_inc(mem_in, 16)
            pool.dma_start(sec(17), A["windows"]).then_inc(mem_in, 16)
            for l in range(DEPTH):
                GC.enter(f"X{l}")
                if l == 0:
                    pool.wait_ge(vec_done, VC.at("mem.n", "AB"))
                    pool.wait_ge(act_done, SC.at("memT", "AB"))
                else:
                    pool.wait_ge(pe_done, PC.at("end", "X0"))
                mem_gain(COL_F[l] + 8, feat(18, 2), cols2)

        @block.scalar
        def _(act):
            def link(ins, *names):
                ins.then_inc(act_done, SC(*names))
                act.wait_ge(act_done, SC.n)

            units = Units()

            def emit(r, use, q, _):
                act.wait_ge(raw_full[r], units.count(16 * LAYER_UNITS // RAW, 16 * use))
                act.wait_ge(split_free[q % SPLIT], units.count(LAYER_SPLIT // SPLIT, q // SPLIT + 1))
                nc.scalar.activation(w_hi[:, q % SPLIT, :], raw[:, r, :], ACT.Copy).then_inc(hi_done[q % SPLIT], 1)

            split = splitter(act, SC, units, emit)

            def filled(name, i=0):
                split(PC.split_at((name, i)), AHEAD, PC.unit_at((name, i)))
                act.wait_ge(pe_done, PC.at((name, i)))
                return bank(SC, name, i)

            def after_vec(name, stage=None):
                split(VC.split_at(name, stage))
                return VC.at(name, stage)

            def copy(dst, name, i, func=ACT.Copy, *marks, view=None, **kw):
                b = filled(name, i)
                link(nc.scalar.activation(dst, (view(b) if view else b[:, :]), func, **kw), ("free", name, i), *marks)

            def rstd(name, n):
                act.wait_ge(vec_done, after_vec(name + ".ms"))
                link(nc.scalar.activation(st[:, 1, 0:n], st[:, 0, 0:n], ACT.Ln))
                link(nc.scalar.activation(st[:, 1, 0:n], st[:, 1, 0:n], ACT.Exp, scale=-0.5), name + ".rstd")

            def sums(src, name):
                for t in range(NT):
                    link(nc.scalar.activation(sec(22), src[:, t, :], ACT.Square, accum_out=st[:, 0, t:t + 1]),
                         *([name + ".ss"] if t else []))

            def norm_T(col, c, name="h"):
                sums(xs, name)
                rstd(name, NT)
                gains(col, c)

            def gains(col, c):
                for i in range(4):
                    b = halves(filled("hT", i))
                    for j in range(2):
                        k = 2 * i + j
                        link(nc.scalar.activation(h_hi[:, k, :], b[:, j, :], ACT.Copy, scale=c[:, col + k:col + k + 1]),
                             *(["hT%d" % i] if j else []))

            SC.enter("pro")
            units.enter(None, [])
            act.wait_ge(mem_in, 32)
            act.wait_ge(pool_done, GC.at("eps", "pro"))
            m = arena[:, 0:2, :]
            sums(m, "mem")
            rstd("mem", NT)
            act.wait_ge(vec_done, after_vec("trig.in"))
            link(nc.scalar.activation(trig[:, :, :, :], arena[:, 4, 0:256].rearrange("p (a t n) -> p a t n", a=2, t=2),
                                      ACT.Sin), "trig")
            for i in range(4):
                copy(memT[:, 2 * i:2 * i + 2, :], "memT", i, view=halves)
            act.wait_ge(x_in, 16)
            act.wait_ge(pe_done, PC.at("end"))
            act.wait_ge(vec_done, after_vec("end"))
            act.sem_inc(arrived, 1)
            act.wait_ge(arrived, 3)
            act.sem_clear(act_done)
            act.sem_clear(pe_done)
            act.sem_clear(vec_done)
            act.sem_clear(pool_done)
            act.sem_clear(arrived)
            act.sem_inc(go, 1)

            with act.Fori(0, DEPTH) as l:
                SC.enter("L", True)
                SC.split = 0
                units.enter(l, LPLAN)
                act.wait_ge(go, l + 1)
                act.sem_inc(spare, 1)
                copy(cols[:, :], "cols", 0, ACT.Copy, "cols", view=lambda b: b[:, 0:52])
                norm_T(0, cols)
                for i in range(2):
                    copy(feat(0)[:, 2 * i:2 * i + 2, :], "sbq", i, ACT.Copy, f"sbq{i}", view=halves, scale=HD ** -0.5)
                for i in range(2):
                    copy(feat(1)[:, 2 * i:2 * i + 2, :], "sbk", i, ACT.Copy, f"sbk{i}", view=halves)
                for t in range(NT):
                    copy(tok(2)[:, t, :], "sbv", t, ACT.Copy, f"sbv{t}")
                for t in range(NT):
                    copy(tok(3)[:, t, :], "sbz", t, ACT.Silu, f"sbz{t}")
                for i in range(2):
                    copy(feat(4)[:, 2 * i:2 * i + 2, :], "mk", i, ACT.Copy, f"mk{i}", view=halves)
                for t in range(NT):
                    copy(tok(5)[:, t, :], "mv", t, ACT.Copy, f"mv{t}")
                sbr = sec(13, 2)
                for h in range(H):
                    e = sbr[:, h * TRI:(h + 1) * TRI]
                    b = filled("sbs", h)
                    link(nc.scalar.activation(e, b[:, 0:TRI], ACT.Abs))
                    link(nc.scalar.activation(e, e, ACT.Exp, scale=-1.0))
                    link(nc.scalar.activation(e, e, ACT.Ln, bias=1.0), f"sbln{h}")
                for n, (name, s) in enumerate((("mlq", 11), ("mlk", 12))):
                    for i in range(2):
                        b = halves(filled(name, i))
                        for j in range(2):
                            ft = 2 * i + j
                            c = 16 + 16 * n + 12 + ft
                            link(nc.scalar.activation(feat(s)[:, ft, :], b[:, j, :], ACT.Copy, scale=cols[:, c:c + 1]),
                                 f"{name}.tap{ft}")
                for h in range(H):
                    e = sbr[:, h * TRI:(h + 1) * TRI]
                    act.wait_ge(vec_done, after_vec(f"sblog{h}"))
                    link(nc.scalar.activation(e, e, ACT.Exp), f"sbw{h}")
                for name, s in (("mlq", 11), ("mlk", 12)):
                    act.wait_ge(vec_done, after_vec(name + ".conv"))
                    link(nc.scalar.activation(sec(s), sec(s), ACT.Silu), name)
                for t in range(NT):
                    copy(tok(8)[:, t, :], "mlv", t, ACT.Copy, f"mlv{t}")
                for t in range(NT):
                    copy(tok(9)[:, t, :], "mlo", t, ACT.Sigmoid)
                for t in range(NT):
                    copy(tok(10)[:, t, :], "mlz", t, ACT.Silu, *(["mlz"] if t else []))
                copy(ifc[:, :, :], "mlif", 0, ACT.Copy, "mlif", view=lambda b: b[:, 0:16].rearrange("p (t n) -> p t n", t=2))
                act.wait_ge(vec_done, after_vec("mlf"))
                link(nc.scalar.activation(gr[:, 1, :], gr[:, 0, :], ACT.Abs))
                link(nc.scalar.activation(gr[:, 1, :], gr[:, 1, :], ACT.Exp, scale=-1.0))
                link(nc.scalar.activation(gr[:, 1, :], gr[:, 1, :], ACT.Ln, bias=1.0), "mlf.ln")
                for name, s in (("rtq", 0), ("rtk", 1)):
                    for t in range(NT):
                        copy(tok(s)[:, t, :], name, t, ACT.Copy, f"{name}{t}")
                for t in range(NT):
                    copy(tok(6)[:, t, :], "rtv", t, ACT.Copy, f"rtv{t}")
                for t in range(NT):
                    copy(tok(7)[:, t, :], "rtz", t, ACT.Silu, f"rtz{t}")
                b = filled("mle")
                link(nc.scalar.activation(st[:, 2, :], b[:, 0:8], ACT.Exp))
                link(nc.scalar.activation(st[:, 3, :], b[:, 8:16], ACT.Copy), ("free", "mle", 0), "mlem")
                mlr = sec(15, 2)
                for h in range(H):
                    b = filled("mld", h)
                    o = h * TRI
                    link(nc.scalar.activation(mlr[:, o:o + S], b[:, 0:S], ACT.Exp, bias=st[:, 3, h:h + 1]))
                    link(nc.scalar.activation(mlr[:, o + S:o + TRI], b[:, S:TRI], ACT.Exp, bias=st[:, 3, H + h:H + h + 1]),
                         ("free", "mld", h), f"mld{h}")
                for name, s in (("gmu", 19), ("gmv", 20)):
                    for t in range(NT):
                        copy(tok(s)[:, t, :], name, t, ACT.Gelu_apprx_tanh, f"{name}{t}")

                def head_norm(name):
                    act.wait_ge(vec_done, after_vec(name + ".cen"))
                    act.wait_ge(pool_done, GC.at("mloz"))
                    link(nc.scalar.activation(sec(9), sec(22), ACT.Square), name + ".sq")
                    rstd(name, 8)

                copy(st[:, 3, :], "mln", 0, ACT.Abs, "mln.abs", view=lambda b: b[:, 0:8])
                head_norm("ml")
                for t in range(NT):
                    copy(tok(21)[:, t, :], "gmz", t, ACT.Silu, f"gmz{t}")
                for name, s in (("rqT", 0), ("rkT", 1)):
                    for i in range(2):
                        copy(feat(s)[:, 2 * i:2 * i + 2, :], name, i, ACT.Copy, f"{name}{i}", view=halves)
                rstd("gm", 2)
                for i in range(2):
                    copy(feat(2)[:, 2 * i:2 * i + 2, :], "xaq", i, ACT.Copy, f"xaq{i}", view=halves)
                for t in range(NT):
                    copy(tok(17)[:, t, :], "xaz", t, ACT.Silu, f"xaz{t}")
                head_norm("rt")
                pr = sec(15, 2)
                for h in range(H):
                    act.wait_ge(vec_done, after_vec(f"xamax{h}"))
                    b = filled("xas", h)
                    for t in range(NT):
                        link(nc.scalar.activation(pr[:, h * 512 + t * S:h * 512 + (t + 1) * S], b[:, t * S:(t + 1) * S], ACT.Exp,
                                                  scale=HD ** -0.5, bias=st[:, 4, 2 * h + t:2 * h + t + 1],
                                                  accum_out=st[:, 5, 2 * h + t:2 * h + t + 1]),
                             *([("free", "xas", h), f"xae{h}"] if t else []))

                def gates(b):
                    g = sec(8 if b % 2 == 0 else 19, 2).rearrange("p (t n) -> p t n", t=NT)
                    for i in range(2):
                        copy(feat(23)[:, 2 * i:2 * i + 2, :], f"yT{b}", i, ACT.Copy, *([f"yT{b}"] if i else []), view=halves)
                    if b >= 2:
                        act.wait_ge(vec_done, after_vec(f"merge{b - 2}"))
                    elif b == 0:
                        act.wait_ge(pool_done, GC.at("mloz"))
                    else:
                        act.wait_ge(vec_done, after_vec("gmy"))
                    for i in range(4):
                        n, t = divmod(i, 2)
                        copy(g[:, t, n * 512:(n + 1) * 512], f"gate{b}", i, ACT.Sigmoid, *([f"gate{b}"] if i == 3 else []))

                gates(0)
                for h in range(H):
                    copy(sec(13, 2)[:, h * 512:(h + 1) * 512], "xap", h, ACT.Copy, f"xap{h}")
                for b in range(1, 5):
                    gates(b)
                for i in range(4):
                    copy(feat(0, 2)[:, 2 * i:2 * i + 2, :], "mgT", i, ACT.Copy, *(["mgT"] if i == 3 else []), view=halves)
                o = sec(6, 2).rearrange("p (t n) -> p t n", t=NT)
                for i in range(4):
                    n, t = divmod(i, 2)
                    copy(o[:, t, n * 512:(n + 1) * 512], "o", i, ACT.Copy)
                sums(o, "post")
                rstd("post", NT)
                act.wait_ge(act_done, SC.n)
                act.sem_inc(arrived, 1)

            def plain_norm(col, name="h"):
                norm_T(col, cols2, name)

            assert known is None or SC.split == LAYER_SPLIT
            SC.enter("AB", True)
            SC.split = 0
            units.enter(None, RPLAN)
            act.wait_ge(go, DEPTH + 1)
            act.sem_inc(spare, 1)
            for i, (c, n) in enumerate(((0, COL_F[1]), (COL_F[1], 120))):
                b = filled("cols2", i)
                link(nc.scalar.activation(cols2[:, c:c + n], b[:, 0:n], ACT.Copy), ("free", "cols2", i), f"cols2{i}")
            link(nc.scalar.activation(lam[:, 0, :], cols2[:, COL_AB + 64:COL_AB + 72], ACT.Abs))
            link(nc.scalar.activation(lam[:, 0, :], lam[:, 0, :], ACT.Exp, scale=-1.0))
            link(nc.scalar.activation(lam[:, 0, :], lam[:, 0, :], ACT.Ln, bias=1.0), "lam.ln")
            plain_norm(COL_AB)
            for i in range(4):
                b = halves(filled("rec", i))
                for j in range(2):
                    ft = 2 * i + j
                    link(nc.scalar.activation(feat(2, 2)[:, ft, :], b[:, j, :], ACT.Identity,
                                              scale=cols2[:, COL_AB + 8 + 24 + ft:COL_AB + 8 + 25 + ft],
                                              bias=cols2[:, COL_AB + 40 + ft:COL_AB + 41 + ft]), f"rec.tap{ft}")
            act.wait_ge(mem2_in, 16)
            sums(arena[:, 18:20, :], "mem")
            rstd("mem", NT)
            for i in range(4):
                copy(memT[:, 2 * i:2 * i + 2, :], "memT", i, ACT.Copy, *(["memT"] if i == 3 else []), view=halves)
            for name, s, c in (("ga", 6, COL_AB + 56), ("gx", 4, COL_AB + 48)):
                for i in range(4):
                    b = halves(filled(name, i))
                    for j in range(2):
                        ft = 2 * i + j
                        link(nc.scalar.activation(feat(s, 2)[:, ft, :], b[:, j, :], ACT.Sigmoid, bias=cols2[:, c + ft:c + ft + 1]),
                             *([("free", name, i), f"{name}{i}"] if j else []))
            for i in range(4):
                copy(feat(0, 2)[:, 2 * i:2 * i + 2, :], "gate", i, ACT.Gelu_apprx_tanh, *(["gate"] if i == 3 else []), view=halves)
            act.wait_ge(vec_done, after_vec("lam"))
            for k in range(KD):
                link(nc.scalar.activation(feat(8, 2)[:, k, :], feat(6, 2)[:, k, :], ACT.Tanh, scale=lam[:, 3, k:k + 1]))
            for k in range(KD):
                link(nc.scalar.activation(feat(6, 2)[:, k, :], feat(6, 2)[:, k, :], ACT.Exp, scale=lam[:, 2, k:k + 1]),
                     *(["a"] if k == KD - 1 else []))
            for i in range(2):
                copy(feat(12)[:, 2 * i:2 * i + 2, :], "pu", i, ACT.Copy, *(["pu"] if i else []), view=halves)
            act.wait_ge(vec_done, after_vec("mult2"))
            link(nc.scalar.activation(sec(8, 2), sec(8, 2), ACT.Sqrt), "mult")
            link(nc.scalar.activation(epsc[:, :], epsc[:, :], ACT.Copy), "end")

            def keys_values():
                for i in range(4):
                    copy(feat(14, 2)[:, 2 * i:2 * i + 2, :], "k", i, ACT.Copy, view=halves)
                v = sec(16, 2).rearrange("p (t n) -> p t n", t=NT)
                for i in range(4):
                    n, t = divmod(i, 2)
                    copy(v[:, t, n * 512:(n + 1) * 512], "v", i, ACT.Copy)

            def cross(l):
                SC.enter(f"X{l}")
                act.wait_ge(vec_done, after_vec("end", "AB" if l == 0 else "C"))
                if l == 0:
                    sums(xs, "h")
                    rstd("h", NT)
                    keys_values()
                    gains(COL_F[l], cols2)
                else:
                    plain_norm(COL_F[l])
                for i in range(4):
                    copy(feat(0, 2)[:, 2 * i:2 * i + 2, :], "q", i, ACT.Copy, *(["q"] if i == 3 else []), view=halves)
                pr = sec(6, 2)
                for h in range(H):
                    act.wait_ge(vec_done, after_vec(f"max{h}"))
                    b = filled("s", h)
                    for t in range(NT):
                        link(nc.scalar.activation(pr[:, h * 512 + t * S:h * 512 + (t + 1) * S], b[:, t * S:(t + 1) * S], ACT.Exp,
                                                  scale=1.0 / 16, bias=st[:, 4, 2 * h + t:2 * h + t + 1],
                                                  accum_out=st[:, 5, 2 * h + t:2 * h + t + 1]),
                             *([("free", "s", h), f"e{h}"] if t else []))
                for h in range(H):
                    copy(sec(8, 2)[:, h * 512:(h + 1) * 512], "p", h, ACT.Copy, f"pT{h}")
                for h in range(H):
                    copy(feat(10, 2)[:, 2 * h:2 * h + 2, :], "oT", h, ACT.Copy, *(["oT"] if h == 3 else []), view=halves)

            def ffn(l):
                SC.enter(f"F{l}")
                act.wait_ge(vec_done, after_vec("end", f"X{l}"))
                plain_norm(COL_F[l] + 16)
                w0, b0 = COL_F[l] + 24, COL_F[l] + 96
                for j in range(6):
                    c = feat(6 + j % 2)
                    if j >= 2:
                        act.wait_ge(vec_done, after_vec(f"h{j - 2}"))
                    for i in range(2):
                        b = halves(filled(f"g{j}", i))
                        for q in range(2):
                            f, ft = 2 * i + q, 4 * j + 2 * i + q
                            link(nc.scalar.activation(c[:, f, :], b[:, q, :], ACT.Identity, scale=cols2[:, w0 + 48 + ft:w0 + 49 + ft],
                                                      bias=cols2[:, b0 + ft:b0 + ft + 1]), f"tap{ft}")
                    act.wait_ge(vec_done, after_vec(f"conv{j}"))
                    link(nc.scalar.activation(sec(6 + j % 2), sec(6 + j % 2), ACT.Gelu_apprx_tanh), f"gelu{j}")

            cross(0)
            ffn(0)
            SC.enter("C")
            act.wait_ge(vec_done, after_vec("end", "F0"))
            plain_norm(COL_C)
            for i in range(4):
                b = halves(filled("cb", i))
                for j in range(2):
                    ft = 2 * i + j
                    c = COL_C + 16 + ft
                    link(nc.scalar.activation(feat(0, 2)[:, ft, :], b[:, j, :], ACT.Sigmoid, bias=cols2[:, c:c + 1]),
                         *([("free", "cb", i), f"cb{i}"] if j else []))
            w0 = COL_C + 48
            for ft in range(KD):
                act.wait_ge(vec_done, after_vec(f"glu{ft}"))
                link(nc.scalar.activation(feat(4, 2)[:, ft, :], feat(2, 2)[:, ft, :], ACT.Identity,
                                          scale=cols2[:, w0 + 240 + ft:w0 + 241 + ft], bias=cols2[:, COL_C + 24 + ft:COL_C + 25 + ft]),
                     f"tap{ft}")
            keys_values()
            act.wait_ge(vec_done, after_vec("cen"))
            link(nc.scalar.activation(sec(8, 2), sec(6, 2), ACT.Square), "sq")
            act.wait_ge(vec_done, after_vec("var"))
            link(nc.scalar.activation(sec(13)[:, 0:S], sec(13)[:, 0:S], ACT.Ln))
            link(nc.scalar.activation(sec(13)[:, 0:S], sec(13)[:, 0:S], ACT.Exp, scale=-0.5), "rstd")
            act.wait_ge(vec_done, after_vec("xhat"))
            for ft in range(KD):
                link(nc.scalar.activation(feat(10, 2)[:, ft, :], feat(6, 2)[:, ft, :], ACT.Silu,
                                          scale=cols2[:, COL_C + 32 + ft:COL_C + 33 + ft], bias=cols2[:, COL_C + 40 + ft:COL_C + 41 + ft]),
                     *(["silu"] if ft == KD - 1 else []))
            link(nc.scalar.activation(epsc[:, :], epsc[:, :], ACT.Copy), "end")
            cross(1)
            ffn(1)
            act.wait_ge(vec_done, after_vec("res"))
            sums(xs, "fin")
            rstd("fin", NT)

        @block.vector
        def _(dve):
            def link(ins, *names):
                ins.then_inc(vec_done, VC(*names))
                dve.wait_ge(vec_done, VC.n)

            tt, ts, stt = nc.vector.tensor_tensor, nc.vector.tensor_scalar, nc.vector.scalar_tensor_tensor

            units = Units()

            def emit(r, use, q, _):
                dve.wait_ge(hi_done[q % SPLIT], units.count(LAYER_SPLIT // SPLIT, q // SPLIT + 1))
                tt(w_lo[:, q % SPLIT, :], raw[:, r, :], w_hi[:, q % SPLIT, :].bitcast(F32), ALU.subtract)\
                    .then_inc(split_full[q % SPLIT], 1)

            split = splitter(dve, VC, units, emit)

            def filled(name, i=0):
                split(PC.split_at((name, i)), AHEAD, PC.unit_at((name, i)))
                dve.wait_ge(pe_done, PC.at((name, i)))
                return bank(VC, name, i)

            def after_act(name, stage=None):
                split(SC.split_at(name, stage))
                return SC.at(name, stage)

            def mean_square(name, n, width):
                dve.wait_ge(act_done, after_act(name + ".ss"))
                link(ts(st[:, 0, 0:n], st[:, 0, 0:n], 1.0 / width, EPS, ALU.mult, ALU.add), name + ".ms")

            def low_part(col, c):
                for i in range(4):
                    b = halves(filled("hT", i))
                    dve.wait_ge(act_done, after_act("hT%d" % i))
                    for j in range(2):
                        k = 2 * i + j
                        link(stt(h_lo[:, k, :], b[:, j, :], c[:, col + k:col + k + 1], h_hi[:, k, :].bitcast(F32),
                                 ALU.mult, ALU.subtract), *([("free", "hT", i), "h_lo%d" % i] if j else []))

            def normalise(src, dst, name, mark):
                mean_square(name, NT, D)
                dve.wait_ge(act_done, after_act(name + ".rstd"))
                for t in range(NT):
                    link(ts(dst[:, t, :], src[:, t, :], st[:, 1, t:t + 1], None, ALU.mult), *([mark] if t else []))

            VC.enter("pro")
            units.enter(None, [])
            xn = arena[:, 22:24, :]
            normalise(arena[:, 0:2, :], arena[:, 2:4, :], "mem", "mem.n")
            dve.wait_ge(mem_in, 32)
            dve.wait_ge(const_in, 16)
            link(nc.vector.tensor_copy(pos_f[:, :], pos_i[:, :]))
            ang, n, r = (arena[:, 5, a * 128:(a + 1) * 128].rearrange("p (t n) -> p t n", t=2) for a in range(3))
            cs = arena[:, 4, 0:256].rearrange("p (a t n) -> p a t n", a=2, t=2)
            for t in range(NT):
                link(ts(ang[:, t, :], con(C_INV, 64), pos_f[:, t:t + 1], None, ALU.mult))
            MAGIC = 1.5 * 2.0 ** 23
            link(ts(n, ang, float(1 / (2 * np.pi)), MAGIC, ALU.mult, ALU.add))
            link(ts(n, n, MAGIC, None, ALU.subtract))
            c1_ = 6.28125
            c2_ = float(np.float32(np.round((2 * np.pi - c1_) * 2 ** 20) / 2 ** 20))
            c3_ = float(2 * np.pi - c1_ - c2_)
            link(stt(r, n, -c1_, ang, ALU.mult, ALU.add))
            link(stt(r, n, -c2_, r, ALU.mult, ALU.add))
            link(stt(r, n, -c3_, r, ALU.mult, ALU.add))
            PI = 3.1415925
            link(ts(cs[:, 1], r, PI, -PI, ALU.min, ALU.max))
            link(ts(r, r, float(np.pi / 2), None, ALU.add))
            link(ts(n, r, float(np.pi), float(-2 * np.pi), ALU.is_gt, ALU.mult))
            link(tt(r, r, n, ALU.add))
            link(ts(cs[:, 0], r, PI, -PI, ALU.min, ALU.max), "trig.in")
            dve.wait_ge(act_done, after_act("trig"))
            link(ts(pos_f[:, :], pos_f[:, :], 1.0, None, ALU.mult), "end")
            dve.sem_inc(arrived, 1)

            with dve.Fori(0, DEPTH) as l:
                VC.enter("L", True)
                VC.split = 0
                units.enter(l, LPLAN)
                dve.wait_ge(go, l + 1)
                dve.sem_inc(spare, 1)
                normalise(xs, xn, "h", "xn")
                low_part(0, cols)
                sbr = sec(13, 2)
                for h in range(H):
                    e = sbr[:, h * TRI:(h + 1) * TRI]
                    b = bank(VC, "sbs", h)
                    dve.wait_ge(act_done, after_act(f"sbln{h}"))
                    link(stt(e, b[:, 0:TRI], 0.0, e, ALU.max, ALU.add))
                    link(tt(e, e, con(C_LKM, TRI), ALU.mult), f"sblk{h}")
                for n, (name, s) in enumerate((("mlq", 11), ("mlk", 12))):
                    for i in range(2):
                        b = halves(filled(name, i))
                        for j in range(2):
                            ft = 2 * i + j
                            dve.wait_ge(act_done, after_act(f"{name}.tap{ft | 1}"))
                            for d in range(1, 4):
                                c = 16 + 16 * n + 4 * (3 - d) + ft
                                y = feat(s)[:, ft, d:S]
                                marks = [("free", name, i)] if d == 3 and j == 1 else []
                                if marks and i == 1:
                                    marks.append(name + ".conv")
                                link(stt(y, b[:, j, 0:S - d], cols[:, c:c + 1], y, ALU.mult, ALU.add), *marks)
                for h in range(H):
                    e = sbr[:, h * TRI:(h + 1) * TRI]
                    b = filled("sbw", h)
                    link(stt(e, b[:, 0:TRI], 0.0, con(C_NB, TRI), ALU.min, ALU.add), f"sblog{h}", ("free", "sbw", h))
                for t in range(NT):
                    b = filled("sby", t)
                    dve.wait_ge(act_done, after_act(f"sbz{t}"))
                    link(tt(tok(3)[:, t, :], b[:, :], tok(3)[:, t, :], ALU.mult), ("free", "sby", t), f"y0{t}")
                b = filled("mlifT")
                dve.wait_ge(small_in, (l + 1) * (2 * 16))
                link(ts(gr[:, 0, :], b[0:H, S:2 * S], bif[:, 1:2], None, ALU.add), "mlf")
                link(ts(gr[:, 2, :], b[0:H, 0:S], bif[:, 0:1], None, ALU.add), ("free", "mlifT", 0))
                dve.wait_ge(act_done, after_act("mlf.ln"))
                link(stt(gr[:, 0, :], gr[:, 0, :], 0.0, gr[:, 1, :], ALU.min, ALU.subtract))
                link(ts(gr[:, 1, :], gr[:, 0, :], 0.0, 1.0, ALU.mult, ALU.add))
                link(nc.vector.tensor_tensor_scan(gr[:, 3, :], gr[:, 1, :], gr[:, 0, :], 0.0, ALU.mult, ALU.add))
                link(tt(gr[:, 2, :], gr[:, 2, :], gr[:, 3, :], ALU.subtract))
                link(nc.vector.tensor_tensor_scan(gr[:, 1, :], gr[:, 2, :], gr[:, 2, :], 0.0, ALU.max, ALU.max))
                link(ts(gr[:, 0, :], gr[:, 1, :], -1.0, None, ALU.mult))
                link(tt(gr[:, 3, :], gr[:, 0, :], gr[:, 3, :], ALU.subtract), "mlrows")
                cosv, sinv = (trig[:, a].unsqueeze(2).to_broadcast([P, NT, H, 64]) for a in range(2))
                for name, s, d in (("rtq", 0, 17), ("rtk", 1, 18)):
                    dve.wait_ge(act_done, after_act(name + "1"))
                    x1, x2 = tok4(s)[:, :, :, 0:64], tok4(s)[:, :, :, 64:128]
                    y1, y2 = tok4(d)[:, :, :, 0:64], tok4(d)[:, :, :, 64:128]
                    t1, t2 = tok4(22)[:, :, :, 0:64], tok4(22)[:, :, :, 64:128]
                    for t in range(NT):
                        link(tt(t1[:, t], x2[:, t], sinv[:, t], ALU.mult))
                        link(tt(y1[:, t], x1[:, t], cosv[:, t], ALU.mult))
                        link(tt(y1[:, t], y1[:, t], t1[:, t], ALU.subtract))
                        link(tt(t2[:, t], x2[:, t], cosv[:, t], ALU.mult))
                        link(tt(y2[:, t], x1[:, t], sinv[:, t], ALU.mult))
                        link(tt(y2[:, t], y2[:, t], t2[:, t], ALU.add), *([name + "r"] if t else []))
                mlr = sec(15, 2)
                for h in range(H):
                    e = mlr[:, h * TRI:(h + 1) * TRI]
                    b = filled("mls", h)
                    dve.wait_ge(act_done, after_act(f"mld{h}"))
                    link(stt(e, b[:, 0:TRI], HD ** -0.5, e, ALU.mult, ALU.mult), f"mlsc{h}", ("free", "mls", h))
                dve.wait_ge(act_done, after_act("mln.abs"))
                link(tt(st[:, 2, :], st[:, 3, :], st[:, 2, :], ALU.max))
                link(nc.vector.reciprocal(st[:, 2, :], st[:, 2, :]))

                def head_norm(name, gate):
                    hb = sec(22).rearrange("p (g n) -> p g n", g=8)
                    link(nc.vector.tensor_reduce(st[:, 6, :], hb, AX.X, ALU.add))
                    link(ts(st[:, 6, :], st[:, 6, :], 1.0 / HD, None, ALU.mult))
                    link(tt(hb, hb, st[:, 6, :].unsqueeze(2).to_broadcast([P, 8, HD]), ALU.subtract), name + ".cen")
                    dve.wait_ge(act_done, after_act(name + ".sq"))
                    link(nc.vector.tensor_reduce(st[:, 6, :], sec(9).rearrange("p (g n) -> p g n", g=8), AX.X, ALU.add))
                    link(ts(st[:, 0, :], st[:, 6, :], 1.0 / HD, EPS, ALU.mult, ALU.add), name + ".ms")
                    dve.wait_ge(act_done, after_act(name + ".rstd"))
                    link(tt(hb, hb, st[:, 1, :].unsqueeze(2).to_broadcast([P, 8, HD]), ALU.mult))
                    link(tt(sec(gate), sec(gate), sec(22), ALU.mult), name + ".y")

                for t in range(NT):
                    b = quarters(filled("mly", t))
                    link(tt(tok4(22)[:, t], b, st[:, 2, 4 * t:4 * t + 4].unsqueeze(2).to_broadcast([P, H, HD]), ALU.mult),
                         ("free", "mly", t))
                dve.wait_ge(pool_done, GC.at("mloz"))
                head_norm("ml", 10)
                for t in range(NT):
                    dve.wait_ge(act_done, after_act(f"gmv{t}"))
                    link(nc.vector.bn_stats(bst[:, 0, 0:6], tok(20)[:, t, :]))
                    link(nc.vector.bn_aggr(st[:, 7, 2 * t:2 * t + 2], bst[:, 0, 0:6]))
                for t in range(NT):
                    link(ts(st[:, 0, t:t + 1], st[:, 7, 2 * t + 1:2 * t + 2], EPS, None, ALU.add), *(["gm.ms"] if t else []))
                for h in range(H):
                    e = sbr[:, h * TRI:(h + 1) * TRI]
                    b = filled("rts", h)
                    dec = con(C_DEC + 2 * P * h, 2 * P)
                    link(tt(e[:, 0:S], b[:, 0:S], dec, ALU.mult))
                    link(tt(e[:, S:TRI], b[:, S:TRI], dec[:, 0:P], ALU.mult), f"rtsc{h}", ("free", "rts", h))
                dve.wait_ge(act_done, after_act("gm.rstd"))
                for t in range(NT):
                    link(ts(tok(20)[:, t, :], tok(20)[:, t, :], st[:, 7, 2 * t:2 * t + 1], st[:, 1, t:t + 1], ALU.subtract, ALU.mult))
                dve.wait_ge(small2_in, (l + 1) * 48)
                for o, op in ((D, ALU.mult), (D + W, ALU.add)):
                    for t in range(NT):
                        link(tt(tok(20)[:, t, :], tok(20)[:, t, :], brow[:, o:o + W], op), *(["gmln"] if t and op == ALU.add else []))
                b = quarters(filled("wsT"))
                link(tt(wsT[:, :, :], b, con(C_GMM).unsqueeze(1).to_broadcast([P, 4, P]), ALU.mult), "wsT", ("free", "wsT", 0))
                for t in range(NT):
                    b = filled("rty", t)
                    link(nc.vector.tensor_copy(tok(22)[:, t, :], b[:, :]), ("free", "rty", t))
                dve.wait_ge(act_done, after_act("rtz1"))
                head_norm("rt", 7)
                for h in range(H):
                    b = halves(filled("xas", h))
                    link(nc.vector.tensor_reduce(st[:, 4, 2 * h:2 * h + 2], b, AX.X, ALU.max))
                    link(ts(st[:, 4, 2 * h:2 * h + 2], st[:, 4, 2 * h:2 * h + 2], -HD ** -0.5, None, ALU.mult), f"xamax{h}")
                for t in range(NT):
                    b = filled("gmy", t)
                    for g in range(4):
                        v = tok4(19)[:, t, g, :]
                        link(stt(v, b[:, g * P:(g + 1) * P], cols[:, 48 + g:49 + g], v, ALU.add, ALU.mult),
                             *([("free", "gmy", t)] if g == 3 else []))
                dve.wait_ge(act_done, after_act("gmz1"))
                link(tt(sec(21), sec(21), sec(19), ALU.mult), "gmy")
                dve.wait_ge(act_done, after_act("xae3"))
                link(nc.vector.reciprocal(st[:, 5, :], st[:, 5, :]))
                mg = sec(11, 2).rearrange("p (t n) -> p t n", t=NT)

                def merge(b):
                    g = sec(8 if b % 2 == 0 else 19, 2).rearrange("p (t n) -> p t n", t=NT)
                    dve.wait_ge(act_done, after_act(f"gate{b}"))
                    for i in range(4):
                        n, t = divmod(i, 2)
                        u = filled(f"up{b}", i)
                        gv, mv = g[:, t, n * 512:(n + 1) * 512], mg[:, t, n * 512:(n + 1) * 512]
                        if b == 0:
                            link(tt(mv, u[:, :], gv, ALU.mult), ("free", f"up{b}", i), *(["merge0"] if i == 3 else []))
                        else:
                            link(tt(gv, u[:, :], gv, ALU.mult), ("free", f"up{b}", i))
                            link(tt(mv, mv, gv, ALU.add), *([f"merge{b}"] if i == 3 else []))

                merge(0)
                merge(1)
                for t in range(NT):
                    b = filled("xay", t)
                    for h in range(H):
                        z = tok4(17)[:, t, h, :]
                        link(stt(z, b[:, h * P:(h + 1) * P], st[:, 5, 2 * h + t:2 * h + t + 1], z, ALU.mult, ALU.mult),
                             *([("free", "xay", t), f"y4{t}"] if h == 3 else []))
                for b in range(2, 5):
                    merge(b)
                mean_square("post", NT, D)
                dve.wait_ge(act_done, after_act("post.rstd"))
                o = sec(6, 2).rearrange("p (t n) -> p t n", t=NT)
                for t in range(NT):
                    link(tt(o[:, t, :], o[:, t, :], brow[:, 0:D], ALU.mult))
                    link(stt(xs[:, t, :], o[:, t, :], st[:, 1, t:t + 1], xs[:, t, :], ALU.mult, ALU.add), *(["res"] if t else []))
                dve.sem_inc(arrived, 1)

            assert known is None or VC.split == LAYER_SPLIT
            VC.enter("AB", True)
            VC.split = 0
            units.enter(None, RPLAN)
            dve.wait_ge(go, DEPTH + 1)
            dve.sem_inc(spare, 1)
            lc = cols2[:, COL_AB + 64:COL_AB + 72]
            dve.wait_ge(act_done, after_act("cols20"))
            link(ts(lam[:, 1, :], lc, -1.0, 0.0, ALU.mult, ALU.max))
            dve.wait_ge(act_done, after_act("lam.ln"))
            link(tt(lam[:, 1, :], lam[:, 1, :], lam[:, 0, :], ALU.add))
            link(ts(lam[:, 2, :], lam[:, 1, :], -8.0, None, ALU.mult))
            link(ts(lam[:, 3, :], lam[:, 1, :], 8.0, None, ALU.mult), "lam")
            normalise(xs, xn, "h", "xn")
            low_part(COL_AB, cols2)
            for i in range(4):
                b = halves(filled("rec", i))
                for j in range(2):
                    ft = 2 * i + j
                    dve.wait_ge(act_done, after_act(f"rec.tap{ft | 1}"))
                    for d in range(1, 4):
                        c = COL_AB + 8 + 8 * (3 - d) + ft
                        y = feat(2, 2)[:, ft, d:S]
                        link(stt(y, b[:, j, 0:S - d], cols2[:, c:c + 1], y, ALU.mult, ALU.add),
                             *([("free", "rec", i), f"xr{i}"] if d == 3 and j == 1 else []))
            dve.wait_ge(mem2_in, 16)
            normalise(arena[:, 18:20, :], arena[:, 20:22, :], "mem", "mem.n")
            dve.wait_ge(act_done, after_act("gx3"))
            link(tt(sec(4, 2), sec(4, 2), sec(2, 2), ALU.mult))
            dve.wait_ge(act_done, after_act("a"))
            split(PC.split_at(("pu", 1)))
            link(ts(sec(10, 2), sec(8, 2), 1.0, None, ALU.add))
            link(nc.vector.reciprocal(sec(10, 2), sec(10, 2)))
            link(stt(sec(8, 2), sec(8, 2), 2.0, sec(10, 2), ALU.mult, ALU.mult), "mult2")
            dve.wait_ge(act_done, after_act("pu"))
            dve.wait_ge(mem_in, 5 * 16)
            src = feat(12)
            for d in range(4):
                w = 2 ** d
                dst = feat(13 + d % 2)
                link(tt(dst[:, d:4, w:S], src[:, d:4, w:S], src[:, d:4, 0:S - w], ALU.add))
                link(nc.vector.tensor_copy(dst[:, d:4, 0:w], src[:, d:4, 0:w]))
                rc = sec(17)[:, d * S:(d + 1) * S]
                link(tt(feat(16)[:, d, :], dst[:, d, :], rc, ALU.mult))
                link(tt(feat(16)[:, d, :], feat(16)[:, d, :], feat(12)[:, d, :], ALU.subtract), *(["pm"] if d == 3 else []))
                src = dst
            dve.wait_ge(act_done, after_act("mult"))
            link(tt(sec(4, 2), sec(4, 2), sec(8, 2), ALU.mult))
            for k in range(KD):
                link(nc.vector.tensor_tensor_scan(feat(10, 2)[:, k, :], feat(6, 2)[:, k, :], feat(4, 2)[:, k, :], 0.0,
                                                  ALU.mult, ALU.add))
            dve.wait_ge(act_done, after_act("gate"))
            link(tt(sec(10, 2), sec(10, 2), sec(0, 2), ALU.mult), "ya")
            for i in range(2):
                b = halves(filled("pl", i))
                for j in range(2):
                    g = 2 * i + j
                    link(ts(feat(15)[:, g, :], b[:, j, :], cols2[:, COL_AB + 72 + g:COL_AB + 73 + g],
                            cols2[:, COL_AB + 76 + g:COL_AB + 77 + g], ALU.add, ALU.mult),
                         *([("free", "pl", i), f"yb{i}"] if j else []))

            def residual(bias=False):
                for i in range(4):
                    n, t = divmod(i, 2)
                    b = filled("o", i)
                    xv = xs[:, t, n * 512:(n + 1) * 512]
                    link(tt(xv, b[:, :], xv, ALU.add), ("free", "o", i))
                    if bias:
                        link(tt(xv, xv, brow[:, n * 512:(n + 1) * 512], ALU.add))
                link(ts(pos_f[:, :], pos_f[:, :], 1.0, None, ALU.mult), "end", "res")

            residual()

            def cross(l):
                VC.enter(f"X{l}")
                normalise(xs, xn, "h", "xn")
                low_part(COL_F[l], cols2)
                for h in range(H):
                    b = halves(filled("s", h))
                    link(nc.vector.tensor_reduce(st[:, 4, 2 * h:2 * h + 2], b, AX.X, ALU.max))
                    link(ts(st[:, 4, 2 * h:2 * h + 2], st[:, 4, 2 * h:2 * h + 2], -1.0 / 16, None, ALU.mult), f"max{h}")
                pr = sec(6, 2)
                for h in range(H):
                    dve.wait_ge(act_done, after_act(f"e{h}"))
                    link(nc.vector.reciprocal(st[:, 5, 2 * h:2 * h + 2], st[:, 5, 2 * h:2 * h + 2]))
                    for t in range(NT):
                        v = pr[:, h * 512 + t * S:h * 512 + (t + 1) * S]
                        link(ts(v, v, st[:, 5, 2 * h + t:2 * h + t + 1], None, ALU.mult), *([f"pn{h}"] if t else []))
                residual()

            def ffn(l):
                VC.enter(f"F{l}")
                normalise(xs, xn, "h", "xn")
                low_part(COL_F[l] + 16, cols2)
                w0 = COL_F[l] + 24
                for j in range(6):
                    c = feat(6 + j % 2)
                    for i in range(2):
                        b = halves(filled(f"g{j}", i))
                        for q in range(2):
                            f, ft = 2 * i + q, 4 * j + 2 * i + q
                            dve.wait_ge(act_done, after_act(f"tap{ft | 1}"))
                            for d in range(1, 3):
                                cc = w0 + 24 * (2 - d) + ft
                                last = d == 2 and q == 1
                                link(stt(c[:, f, d:S], b[:, q, 0:S - d], cols2[:, cc:cc + 1], c[:, f, d:S], ALU.mult, ALU.add),
                                     *([("free", f"g{j}", i)] if last else []), *([f"conv{j}"] if last and i else []))
                    dve.wait_ge(act_done, after_act(f"gelu{j}"))
                    for i in range(2):
                        b = halves(filled(f"u{j}", i))
                        link(tt(feat(j)[:, 2 * i:2 * i + 2, :], b, c[:, 2 * i:2 * i + 2, :], ALU.mult),
                             ("free", f"u{j}", i), *([f"h{j}"] if i else []))
                residual()

            cross(0)
            ffn(0)
            VC.enter("C")
            normalise(xs, xn, "h", "xn")
            low_part(COL_C, cols2)
            for i in range(4):
                b = halves(filled("ca", i))
                dve.wait_ge(act_done, after_act(f"cb{i}"))
                for j in range(2):
                    ft = 2 * i + j
                    link(stt(feat(2, 2)[:, ft, :], b[:, j, :], cols2[:, COL_C + 8 + ft:COL_C + 9 + ft], feat(0, 2)[:, ft, :],
                             ALU.add, ALU.mult), f"glu{ft}", *([("free", "ca", i)] if j else []))
            w0 = COL_C + 48
            for pair in range(KD // 2):
                dve.wait_ge(act_done, after_act(f"tap{2 * pair + 1}"))
                for d in range(1, 31):
                    for ft in (2 * pair, 2 * pair + 1):
                        c = w0 + 8 * (30 - d) + ft
                        y = feat(4, 2)[:, ft, d:S]
                        stt(y, feat(2, 2)[:, ft, 0:S - d], cols2[:, c:c + 1], y, ALU.mult, ALU.add)\
                            .then_inc(vec_done, VC(*([f"dw{ft}"] if d == 30 else [])))
                        dve.wait_ge(vec_done, VC.n - 1)
            dve.wait_ge(vec_done, VC.n)
            b = filled("mu", 0)
            link(ts(sec(13)[:, 0:S], b[:, 0:S], 1.0 / D, None, ALU.mult), ("free", "mu", 0))
            bc = sec(13)[:, 0:S].unsqueeze(1).to_broadcast([P, KD, S])
            link(tt(feat(6, 2), feat(4, 2), bc, ALU.subtract), "cen")
            b = filled("var", 0)
            link(ts(sec(13)[:, 0:S], b[:, 0:S], 1.0 / D, EPS, ALU.mult, ALU.add), ("free", "var", 0), "var")
            dve.wait_ge(act_done, after_act("rstd"))
            link(tt(feat(6, 2), feat(6, 2), bc, ALU.mult), "xhat")
            residual(bias=True)
            cross(1)
            ffn(1)
            normalise(xs, sec(0, 2).rearrange("p (t d) -> p t d", t=NT), "fin", "finn")
            for t in range(NT):
                link(tt(sec(0, 2)[:, t * D:(t + 1) * D], sec(0, 2)[:, t * D:(t + 1) * D], brow[:, D:2 * D], ALU.mult),
                     *(["final"] if t else []))

        @block.tensor
        def _(pe):
            mm = nc.tensor.matmul
            units = Units()
            at = [0]
            fresh = []
            owed = []
            def begin(name, i=0):
                before = BEFORE[PC.stage, name, i]
                if before is not None:
                    key = ("free", *before)
                    if SC.has(key):
                        pe.wait_ge(act_done, SC.at(key))
                    elif VC.has(key):
                        pe.wait_ge(vec_done, VC.at(key))
                    else:
                        assert known is None, key
                return bank(PC, name, i)

            def end(ins, name, i=0):
                ins.then_inc(pe_done, PC((name, i)))

            def give_back():
                while owed:
                    free, n = owed.pop(0)
                    pe.wait_ge(pe_done, n)
                    pe.sem_inc(free, 1)

            def unit(k, m):
                r, use, q, _ = units.plan[at[0]]
                at[0] += 1
                PC.unit = at[0]
                shape = "p (k m) -> p k m"
                if q is None:
                    pe.wait_ge(raw_full[r], units.count(16 * LAYER_UNITS // RAW, 16 * use))
                    return [raw[:, r, 0:k * m].rearrange(shape, k=k)], raw_free[r]
                PC.split += 1
                pe.wait_ge(split_full[q % SPLIT], units.count(LAYER_SPLIT // SPLIT, q // SPLIT + 1))
                return [x[:, q % SPLIT, :].rearrange(shape, k=k) for x in (w_hi, w_lo)], split_free[q % SPLIT]

            def parts(w, src):
                if len(w) == 1:
                    return [(w[0], src)]
                return [(w[0], h_hi), (w[1], h_hi), (w[0], h_lo)]

            def proj_T(name, src=None, i0=0):
                bs = [begin(name, i0 + t) for t in range(NT)]
                for u in range(KD // 2):
                    w, free = unit(2, W)
                    give_back()
                    if fresh:
                        pe.wait_ge(vec_done, VC.at(f"h_lo{u}"))
                    for t in range(NT):
                        for kk in range(2):
                            k = 2 * u + kk
                            for n, (wp, sp_) in enumerate(parts(w, src)):
                                last = k == KD - 1 and n == len(parts(w, src)) - 1
                                ins = mm(bs[t][:, :], sp_[:, k, t * P:(t + 1) * P], wp[:, kk, :], start=k == 0 and n == 0, stop=last)
                        if u == KD // 2 - 1:
                            end(ins, name, i0 + t)
                    if u < KD // 2 - 1:
                        ins.then_inc(free, 1)
                owed.append((free, PC.n))
                fresh.clear()

            def proj_F(name, src=None, i0=0):
                bs = [halves(begin(name, i0 + i)) for i in range(2)]
                for u in range(KD // 2):
                    w, free = unit(2, W)
                    give_back()
                    if fresh:
                        pe.wait_ge(vec_done, VC.at(f"h_lo{u}"))
                    for f in range(4):
                        i, j = divmod(f, 2)
                        for kk in range(2):
                            k = 2 * u + kk
                            for n, (wp, sp_) in enumerate(parts(w, src)):
                                last = k == KD - 1 and n == len(parts(w, src)) - 1
                                ins = mm(bs[i][:, j, :], wp[:, kk, f * P:(f + 1) * P], sp_[:, k, :],
                                         start=k == 0 and n == 0 and j == 0, stop=last, skip_group_check=True)
                        if u == KD // 2 - 1 and j:
                            end(ins, name, i0 + i)
                    if u < KD // 2 - 1:
                        ins.then_inc(free, 1)
                owed.append((free, PC.n))
                fresh.clear()

            def project(kind, name, src=None, i0=0):
                (proj_T if kind == "T" else proj_F)(name, src, i0)

            def wide(name, src, j, chunks):
                bs = [begin(name, i) if j == 0 else bank(PC, name, i) for i in range(4)]
                for k in range(4):
                    w, free = unit(1, D)
                    give_back()
                    last = j == chunks - 1 and k == 3
                    for i in range(4):
                        n, t = divmod(i, 2)
                        ins = mm(bs[i][:, :], src[:, k, t * P:(t + 1) * P], w[0][:, 0, n * 512:(n + 1) * 512],
                                 start=j == 0 and k == 0, stop=last)
                        if last:
                            end(ins, name, i)
                    if not last:
                        ins.then_inc(free, 1)
                if last:
                    owed.append((free, PC.n))

            def turn(name, i, src, cols_per=2):
                b = halves(begin(name, i))
                for j in range(2):
                    for t in range(NT):
                        ins = nc.tensor.transpose(b[:, j, t * P:(t + 1) * P], src[:, t, (2 * i + j) * P:(2 * i + j + 1) * P], ident)
                end(ins, name, i)

            def norm_T():
                pe.wait_ge(vec_done, VC.at("xn"))
                for i in range(4):
                    turn("hT", i, arena[:, 22:24, :])
                fresh.append(True)

            PC.enter("pro")
            pe.wait_ge(const_in, 16)
            pe.wait_ge(vec_done, VC.at("mem.n"))
            for i in range(4):
                turn("memT", i, arena[:, 2:4, :])
            end(nc.tensor.transpose(ps[7][:, 0:P], ident, ident), "endpro")
            for free in raw_free + split_free:
                pe.sem_inc(free, 1)
            pe.wait_ge(pe_done, PC.n)
            PC.marks["pro", "end"] = PC.n
            pe.sem_inc(arrived, 1)

            with pe.Fori(0, DEPTH) as l:
                PC.enter("L", True)
                PC.split = PC.unit = 0
                units.enter(l, LPLAN)
                pe.wait_ge(go, l + 1)
                pe.sem_inc(spare, 1)
                pe.wait_ge(rows_in, (l + 1) * (5 * 16))
                pe.sem_inc(spare, 1)
                b = begin("cols")
                end(nc.tensor.transpose(b[:, 0:52], rows[0:52, :], ident[0:52, 0:52]), "cols")
                norm_T()
                project("F", "sbq")
                project("F", "sbk")
                project("T", "sbv")
                project("T", "sbz")
                pe.wait_ge(pool_done, GC.at("mTg"))
                mTg = feat(15, 2)
                project("F", "mk", mTg)
                project("T", "mv", mTg)

                def scores(name, h, q, k):
                    b = begin(name, h)
                    mm(b[:, 0:S], k[:, h, 0:P], q[:, h, :], start=True, stop=True)
                    end(mm(b[:, S:TRI], k[:, h, P:S], q[:, h, P:S], start=False, stop=True, skip_group_check=True), name, h)

                def mix(name, t, w, v):
                    b = begin(name, t)
                    for h in range(H):
                        o = h * TRI
                        y = b[:, h * HD:(h + 1) * HD]
                        if t == 0:
                            ins = mm(y, w[:, o:o + P], v[:, 0, h * HD:(h + 1) * HD], start=True, stop=True)
                        else:
                            mm(y, w[:, o + P:o + S], v[:, 0, h * HD:(h + 1) * HD], start=True, stop=False)
                            ins = mm(y, w[:, o + S:o + TRI], v[:, 1, h * HD:(h + 1) * HD], start=False, stop=True)
                    end(ins, name, t)

                for h in range(H):
                    scores("sbs", h, feat(0), feat(1))
                project("F", "mlq")
                project("F", "mlk")
                sbr = sec(13, 2)
                for h in range(H):
                    pe.wait_ge(vec_done, VC.at(f"sblk{h}"))
                    b = bank(PC, "sbw", h)
                    e = sbr[:, h * TRI:(h + 1) * TRI]
                    mm(b[:, 0:S], con(C_TRI), e[:, 0:S], start=False, stop=False, skip_group_check=True)
                    mm(b[:, P:S], ones, e[:, S:TRI], start=False, stop=False, skip_group_check=True)
                    end(mm(b[:, S:TRI], con(C_TRI), e[:, S:TRI], start=False, stop=True, skip_group_check=True), "sbw", h)
                project("T", "mlv")
                project("T", "mlo")
                project("T", "mlz")
                (w,), free = unit(KD, 2 * H)
                give_back()
                b = begin("mlif")
                for t in range(NT):
                    for k in range(KD):
                        for n, part in enumerate((h_hi, h_lo)):
                            ins = mm(b[:, t * 2 * H:(t + 1) * 2 * H], part[:, k, t * P:(t + 1) * P].bitcast(F32), w[:, k, :],
                                     start=k == 0 and n == 0, stop=k == KD - 1 and n == 1)
                end(ins, "mlif")
                owed.append((free, PC.n))
                pe.wait_ge(act_done, SC.at("sbw3"))
                for t in range(NT):
                    mix("sby", t, sbr, tok(2))
                pe.wait_ge(act_done, SC.at("mlif"))
                b = begin("mlifT")
                for n in range(2):
                    for t in range(NT):
                        ins = nc.tensor.transpose(b[0:H, n * S + t * P:n * S + (t + 1) * P], ifc[:, t, n * H:(n + 1) * H], ident)
                end(ins, "mlifT")
                for kind, name in ("T", "rtq"), ("T", "rtk"), ("T", "rtv"), ("T", "rtz"):
                    project(kind, name)
                pe.wait_ge(vec_done, VC.at("mlrows"))
                b = begin("mle")
                for n, r in enumerate((3, 2)):
                    for t in range(NT):
                        c = 8 * n + 4 * t
                        ins = nc.tensor.transpose(b[:, c:c + H], gr[0:H, r, t * P:(t + 1) * P], ident[0:H, 0:H])
                end(ins, "mle")
                for h in range(H):
                    b = begin("mld", h)
                    sel = ident[0:H, h:h + 1].to_broadcast([H, P])
                    mm(b[:, 0:S], sel, gr[0:H, 0, :], start=True, stop=False)
                    mm(b[:, 0:P], ident, con(C_MLN), start=False, stop=True)
                    mm(b[:, S:TRI], sel, gr[0:H, 0, P:S], start=True, stop=False)
                    end(mm(b[:, S:TRI], ident, con(C_MLN), start=False, stop=True), "mld", h)
                pe.wait_ge(act_done, SC.at("mlk"))
                for h in range(H):
                    scores("mls", h, feat(11), feat(12))
                project("T", "gmu")
                project("T", "gmv")
                pe.wait_ge(vec_done, VC.at("mlsc3"))
                mlr = sec(15, 2)
                b = begin("mln")
                for h in range(H):
                    o = h * TRI
                    mm(b[:, h:h + 1], mlr[:, o:o + P], ones[:, 0:1], start=True, stop=True)
                    mm(b[:, H + h:H + h + 1], mlr[:, o + P:o + S], ones[:, 0:1], start=True, stop=False)
                    ins = mm(b[:, H + h:H + h + 1], mlr[:, o + S:o + TRI], ones[:, 0:1], start=False, stop=True)
                end(ins, "mln")
                for t in range(NT):
                    mix("mly", t, mlr, tok(8))
                project("T", "gmz")
                for name, s_ in (("rtq", 17), ("rtk", 18)):
                    pe.wait_ge(vec_done, VC.at(name + "r"))
                    for i in range(2):
                        turn({"rtq": "rqT", "rtk": "rkT"}[name], i, tok(s_))
                pe.wait_ge(act_done, SC.at("rkT1"))
                for h in range(H):
                    scores("rts", h, feat(0), feat(1))
                (w,), free = unit(4, P)
                give_back()
                b = quarters(begin("wsT"))
                for g in range(4):
                    ins = nc.tensor.transpose(b[:, g, :], w[:, g, :], ident)
                end(ins, "wsT")
                owed.append((free, PC.n))
                project("F", "xaq")
                project("T", "xaz")
                pe.wait_ge(vec_done, VC.at("rtsc3"))
                for t in range(NT):
                    mix("rty", t, sbr, tok(6))
                pe.wait_ge(act_done, SC.at("xaq1"))
                for h in range(H):
                    b = halves(begin("xas", h))
                    for t in range(NT):
                        ins = mm(b[:, t, :], feat(2)[:, h, t * P:(t + 1) * P], feat(4)[:, h, :], start=True, stop=True)
                    end(ins, "xas", h)
                pe.wait_ge(vec_done, VC.at("gmln"))
                for t in range(NT):
                    b = quarters(begin("gmy", t))
                    for g in range(4):
                        ins = mm(b[:, g, :], wsT[:, g, :], tok4(20)[:, t, g, :], start=True, stop=True)
                    end(ins, "gmy", t)

                YS = [3, 10, 21, 7, 17]

                def gates(b_, ready):
                    pe.wait_ge(vec_done, VC.at(ready))
                    for i in range(2):
                        turn(f"yT{b_}", i, tok(YS[b_]))
                    project("T", f"gate{b_}", i0=0)
                    project("T", f"gate{b_}", i0=2)
                    pe.wait_ge(act_done, SC.at(f"yT{b_}"))
                    wide(f"up{b_}", feat(23), 0, 1)

                gates(0, "y01")
                for h in range(H):
                    pe.wait_ge(act_done, SC.at(f"xae{h}"))
                    b = halves(begin("xap", h))
                    for m in range(2):
                        for t in range(NT):
                            o = h * 512 + t * S + m * P
                            ins = nc.tensor.transpose(b[:, m, t * P:(t + 1) * P], sec(15, 2)[:, o:o + P], ident)
                    end(ins, "xap", h)
                gates(1, "ml.y")
                pe.wait_ge(act_done, SC.at("xap3"))
                for t in range(NT):
                    b = begin("xay", t)
                    for h in range(H):
                        for m in range(2):
                            o = h * 512 + m * S + t * P
                            ins = mm(b[:, h * HD:(h + 1) * HD], sec(13, 2)[:, o:o + P], tok(5)[:, m, h * HD:(h + 1) * HD],
                                     start=m == 0, stop=m == 1)
                    end(ins, "xay", t)
                gates(2, "gmy")
                gates(3, "rt.y")
                gates(4, "y41")
                pe.wait_ge(vec_done, VC.at("merge4"))
                for i in range(4):
                    turn("mgT", i, sec(11, 2).rearrange("p (t n) -> p t n", t=NT))
                pe.wait_ge(act_done, SC.at("mgT"))
                for n in range(2):
                    project("T", "o", feat(0, 2), i0=2 * n)
                give_back()
                pe.wait_ge(pe_done, PC.n)
                pe.sem_inc(arrived, 1)

            assert at[0] == LAYER_UNITS
            at[0] = 0
            PC.split = PC.unit = 0
            units.enter(None, RPLAN)

            def finish():
                PC.marks[PC.stage, "end"] = PC.n

            PC.enter("AB", True)
            pe.wait_ge(go, DEPTH + 1)
            pe.sem_inc(spare, 1)
            pe.wait_ge(rows2_in, ROWS2)
            for i, tiles in enumerate(([(0, 80, 0), (1, 48, COL_C), (2, 124, COL_C + 48), (3, 124, COL_C + 172), (4, 120, COL_F[0])],
                                       [(5, 120, 0)])):
                b = begin("cols2", i)
                for t_, n, c in tiles:
                    ins = nc.tensor.transpose(b[:, c:c + n], rows2[0:n, t_ * P:(t_ + 1) * P], ident[0:n, 0:n])
                end(ins, "cols2", i)
            norm_T()
            project("F", "rec", i0=0)
            project("F", "rec", i0=2)
            pe.wait_ge(vec_done, VC.at("mem.n"))
            for i in range(4):
                turn("memT", i, arena[:, 20:22, :])
            for name in ("ga", "gx"):
                (w,), free = unit(8, P)
                give_back()
                for i in range(4):
                    pe.wait_ge(vec_done, VC.at(f"xr{i}"))
                    b = halves(begin(name, i))
                    for j in range(2):
                        ins = mm(b[:, j, :], w[:, 2 * i + j, :], feat(2, 2)[:, 2 * i + j, :], start=True, stop=True)
                    end(ins, name, i)
                owed.append((free, PC.n))
            project("F", "gate", i0=0)
            project("F", "gate", i0=2)
            project("F", "pu")
            (w,), free = unit(4, P)
            give_back()
            pe.wait_ge(vec_done, VC.at("pm"))
            for i in range(2):
                b = halves(begin("pl", i))
                for j in range(2):
                    ins = mm(b[:, j, :], w[:, 2 * i + j, :], feat(16)[:, 2 * i + j, :], start=True, stop=True)
                end(ins, "pl", i)
            owed.append((free, PC.n))
            pe.wait_ge(vec_done, VC.at("yb1"))

            for j, src in enumerate((feat(10), feat(11), feat(15))):
                wide("o", src, j, 3)
            finish()

            def keys_values(l):
                pe.wait_ge(pool_done, GC.at("mTg", f"X{l}"))
                for kind, name in ("F", "k"), ("T", "v"):
                    for i0 in (0, 2):
                        project(kind, name, feat(18, 2), i0)

            def cross(l):
                PC.enter(f"X{l}")
                if l == 0:
                    pe.wait_ge(vec_done, VC.at("end", "AB"))
                    keys_values(0)
                norm_T()
                project("F", "q", i0=0)
                project("F", "q", i0=2)
                q, k = feat(0, 2), feat(14, 2)
                pe.wait_ge(act_done, SC.at("q"))
                for h in range(H):
                    b = halves(begin("s", h))
                    for t in range(NT):
                        for d in range(2):
                            ins = mm(b[:, t, :], q[:, 2 * h + d, t * P:(t + 1) * P], k[:, 2 * h + d, :], start=d == 0, stop=d == 1)
                    end(ins, "s", h)
                for h in range(H):
                    pe.wait_ge(vec_done, VC.at(f"pn{h}"))
                    b = halves(begin("p", h))
                    for m in range(2):
                        for t in range(NT):
                            o = h * 512 + t * S + m * P
                            ins = nc.tensor.transpose(b[:, m, t * P:(t + 1) * P], sec(6, 2)[:, o:o + P], ident)
                    end(ins, "p", h)
                v = sec(16, 2).rearrange("p (t n) -> p t n", t=NT)
                for h in range(H):
                    pe.wait_ge(act_done, SC.at(f"pT{h}"))
                    b = halves(begin("oT", h))
                    for d in range(2):
                        for m in range(2):
                            c = h * 256 + d * P
                            ins = mm(b[:, d, :], v[:, m, c:c + P], sec(8, 2)[:, h * 512 + m * S:h * 512 + (m + 1) * S],
                                     start=m == 0, stop=m == 1)
                    end(ins, "oT", h)
                pe.wait_ge(act_done, SC.at("oT"))
                for n in range(2):
                    project("T", "o", feat(10, 2), i0=2 * n)
                finish()

            def ffn(l):
                PC.enter(f"F{l}")
                norm_T()
                for j in range(6):
                    project("F", f"g{j}")
                    project("F", f"u{j}")
                    if j:
                        pe.wait_ge(vec_done, VC.at(f"h{j - 1}"))
                        wide("o", feat(j - 1), j - 1, 6)
                pe.wait_ge(vec_done, VC.at("h5"))
                wide("o", feat(5), 5, 6)
                finish()

            cross(0)
            ffn(0)
            PC.enter("C")
            norm_T()
            for name in ("cb", "ca"):
                for i0 in (0, 2):
                    project("F", name, i0=i0)
            keys_values(1)
            b = begin("mu", 0)
            for k in range(KD):
                pe.wait_ge(vec_done, VC.at(f"dw{k}"))
                ins = mm(b[:, 0:S], ones, feat(4, 2)[:, k, :], start=k == 0, stop=k == KD - 1)
            end(ins, "mu", 0)
            pe.wait_ge(act_done, SC.at("sq"))
            b = begin("var", 0)
            for k in range(KD):
                ins = mm(b[:, 0:S], ones, feat(8, 2)[:, k, :], start=k == 0, stop=k == KD - 1)
            end(ins, "var", 0)
            pe.wait_ge(act_done, SC.at("silu"))
            for n in range(2):
                project("T", "o", feat(10, 2), i0=2 * n)
            finish()
            cross(1)
            ffn(1)
            give_back()

    return [C.marks for C in (PC, SC, VC, GC)]


COL_AB, COL_C, COL_F = 0, 80, (376, 496)
ROWS2 = 25 * 16

_INS = ["x", "mem", "positions", "norm_pre", "norm_post", "w_in", "b_igate", "b_fgate", "conv_q", "conv_k", "gm_ln_g",
        "gm_ln_b", "gm_ws", "gm_bs", "mem_norm", "w_mem_kv", "w_up", "w_out", "mem_2", "ab_norm_2", "ab_w_in_2",
        "a_conv_w_2", "a_conv_b_2", "a_gate_x_w_2", "a_gate_x_b_2", "a_gate_a_w_2", "a_gate_a_b_2", "a_lambda_2",
        "b_group_w_2", "b_group_b_2", "b_scale_2", "ab_w_out_2", "c_norm_2", "c_w_pw1_2", "c_b_pw1_2", "c_dw_w_2",
        "c_dw_b_2", "c_ln_g_2", "c_ln_b_2", "c_w_pw2_2", "c_b_pw2_2", "xa_norm_2", "xa_mem_norm_2", "xa_wq_2",
        "xa_wk_2", "xa_wv_2", "xa_wo_2", "f_norm_2", "f_w_up_2", "f_dw_w_2", "f_dw_b_2", "f_w_down_2", "final_norm_2"]


def kernel(**inputs):
    import numpy as _np
    import concourse.bacc as _bacc
    from concourse import mybir as _mybir
    from concourse.bass_utils import run_bass_kernel_spmd as _run

    arrays = {f"in_{n}_dram": _np.ascontiguousarray(inputs[n]) for n in _INS}
    arrays["in_constants_dram"] = constants()
    arrays["in_windows_dram"] = windows()
    known, before = None, ()
    while known != before:
        before = known
        nc = _bacc.Bacc("TRN2", target_bir_lowering=False, num_devices=1)
        A = {n: nc.dram_tensor(f"in_{n}_dram", arrays[f"in_{n}_dram"].shape,
                               _mybir.dt.from_np(arrays[f"in_{n}_dram"].dtype), kind="ExternalInput").ap()
             for n in _INS + ["constants", "windows"]}
        out = nc.dram_tensor("out_0_dram", (1, S, D), F32, kind="ExternalOutput").ap()
        known = build(nc, A, out, known)
    r = _run(nc, [arrays], core_ids=[0])
    return r.results[0]["out_0_dram"]
```
